# Optimizing a Trainium2 kernel written in Bass

```python
import math
import jax, jax.numpy as jnp
from jax import lax
import numpy as np

D_MODEL = 1024
BATCH = 1
SEQ = 256
DEPTH = 2

D_FF = 2816
FFN_HALF = 0.5
DN_HEAD_DIM = 128
DN_HEADS = D_MODEL // 128
DN_WIDTH = DN_HEADS * DN_HEAD_DIM
DN_CONV = 4
DN_CHUNK = 64
SB_HEAD_DIM = 128
SB_HEADS = D_MODEL // 128
SB_WIDTH = SB_HEADS * SB_HEAD_DIM
SB_BLOCK = 128
IN_SIZES = (3 * DN_WIDTH, DN_WIDTH, DN_HEADS, DN_HEADS, SB_WIDTH, SB_WIDTH, SB_WIDTH, D_MODEL, D_MODEL)
N_IN = 4 * DN_WIDTH + 2 * DN_HEADS + 3 * SB_WIDTH + 2 * D_MODEL
RMS_EPS = 1e-6
L2_EPS = 1e-6


def rmsnorm(x, gain):
    xf = x.astype(jnp.float32)
    y = xf * lax.rsqrt(jnp.mean(xf * xf, axis=-1, keepdims=True) + RMS_EPS)
    return (y * gain.astype(jnp.float32)).astype(x.dtype)

def l2norm(x):
    xf = x.astype(jnp.float32)
    return xf * lax.rsqrt(jnp.sum(xf * xf, axis=-1, keepdims=True) + L2_EPS)

def swiglu(h, w_in, w_out):
    gate, up = jnp.split(h @ w_in, 2, axis=-1)
    return (jax.nn.silu(gate) * up) @ w_out

def causal_depthwise_conv(x, w):
    width, ch = w.shape
    return lax.conv_general_dilated(
        x, w[:, None, :], window_strides=(1,), padding=((width - 1, 0),),
        dimension_numbers=("NWC", "WIO", "NWC"), feature_group_count=ch)

def split_cols(proj):
    parts, start = [], 0
    for size in IN_SIZES:
        parts.append(proj[..., start:start + size])
        start += size
    return parts

def to_heads(t, n_heads, head_dim):
    b, s, _ = t.shape
    return t.reshape(b, s, n_heads, head_dim).transpose(0, 2, 1, 3)

def gated_delta_rule_chunked(q, k, v, g, beta):
    b, h, t, dk = q.shape
    dv = v.shape[-1]
    c = DN_CHUNK
    n = t // c
    q = (q * (dk ** -0.5)).reshape(b, h, n, c, dk)
    k = k.reshape(b, h, n, c, dk)
    v = v.astype(jnp.float32).reshape(b, h, n, c, dv)
    beta = beta.reshape(b, h, n, c)
    g = lax.cumsum(g.reshape(b, h, n, c), axis=3)
    idx = jnp.arange(c)
    lower_incl = idx[:, None] >= idx[None, :]
    strict = idx[:, None] > idx[None, :]
    decay = jnp.exp(jnp.where(lower_incl, g[..., :, None] - g[..., None, :], -jnp.inf))
    k_beta = k * beta[..., None]
    lmat = jnp.where(strict, jnp.einsum("bhnid,bhnjd->bhnij", k_beta, k) * decay, 0.0)
    amat = lmat + jnp.eye(c, dtype=jnp.float32)
    rhs = jnp.concatenate([v * beta[..., None], k_beta * jnp.exp(g)[..., None]], axis=-1)
    sol = lax.linalg.triangular_solve(amat, rhs, left_side=True, lower=True, unit_diagonal=True)
    u, w = sol[..., :dv], sol[..., dv:]
    attn_intra = jnp.einsum("bhnid,bhnjd->bhnij", q, k) * decay
    q_dec = q * jnp.exp(g)[..., None]
    g_last = g[..., -1]
    k_dec = k * jnp.exp(g_last[..., None] - g)[..., None]

    def chunk_step(state, inp):
        q_i, k_i, u_i, w_i, a_i, gl_i = inp
        v_new = u_i - jnp.einsum("bhcd,bhdv->bhcv", w_i, state)
        o_i = jnp.einsum("bhcd,bhdv->bhcv", q_i, state) + jnp.einsum("bhij,bhjv->bhiv", a_i, v_new)
        state = state * jnp.exp(gl_i)[..., None, None] + jnp.einsum("bhcd,bhcv->bhdv", k_i, v_new)
        return state, o_i

    chunk_first = lambda arr: jnp.moveaxis(arr, 2, 0)
    s0 = jnp.zeros((b, h, dk, dv), jnp.float32)
    _, o = lax.scan(chunk_step, s0, (chunk_first(q_dec), chunk_first(k_dec), chunk_first(u),
                                     chunk_first(w), chunk_first(attn_intra), chunk_first(g_last)))
    return jnp.moveaxis(o, 0, 2).reshape(b, h, t, dv)

def stick_breaking_attention(q, k, v):
    t = q.shape[2]
    scale = q.shape[-1] ** -0.5
    outs = []
    for blk in range(t // SB_BLOCK):
        t0, t1 = blk * SB_BLOCK, (blk + 1) * SB_BLOCK
        z = jnp.einsum("bhqd,bhkd->bhqk", q[:, :, t0:t1], k[:, :, :t1]).astype(jnp.float32) * scale
        causal = jnp.arange(t1)[None, :] < (t0 + jnp.arange(SB_BLOCK))[:, None]
        log_1mb = jnp.where(causal, -jax.nn.softplus(z), 0.0)
        survive = lax.cumsum(log_1mb, axis=3, reverse=True) - log_1mb
        weights = jnp.where(causal, jnp.exp(jax.nn.log_sigmoid(z) + survive), 0.0)
        outs.append(jnp.einsum("bhqk,bhkd->bhqd", weights.astype(v.dtype), v[:, :, :t1]))
    return jnp.concatenate(outs, axis=2)

def hybrid_mixer(h, w_in, conv_w, a_log, dt_bias, dn_out_norm, sb_q_norm, sb_k_norm,
                 w_branch_a, w_branch_b, w_out):
    b, t, _ = h.shape
    dn_qkv, dn_z, dn_b, dn_a, sb_q, sb_k, sb_v, gate_a, gate_b = split_cols(h @ w_in)
    qkv = jax.nn.silu(causal_depthwise_conv(dn_qkv, conv_w))
    q, k, v = jnp.split(qkv, 3, axis=-1)
    q = l2norm(to_heads(q, DN_HEADS, DN_HEAD_DIM))
    k = l2norm(to_heads(k, DN_HEADS, DN_HEAD_DIM))
    v = to_heads(v, DN_HEADS, DN_HEAD_DIM)
    beta = jax.nn.sigmoid(dn_b.astype(jnp.float32)).transpose(0, 2, 1)
    g = (-jnp.exp(a_log.astype(jnp.float32))
         * jax.nn.softplus(dn_a.astype(jnp.float32) + dt_bias.astype(jnp.float32))).transpose(0, 2, 1)
    o_a = gated_delta_rule_chunked(q, k, v, g, beta).transpose(0, 2, 1, 3)
    o_a = rmsnorm(o_a, dn_out_norm) * jax.nn.silu(dn_z.reshape(b, t, DN_HEADS, DN_HEAD_DIM).astype(jnp.float32))
    y_a = o_a.reshape(b, t, DN_WIDTH).astype(h.dtype) @ w_branch_a
    qb = rmsnorm(to_heads(sb_q, SB_HEADS, SB_HEAD_DIM), sb_q_norm)
    kb = rmsnorm(to_heads(sb_k, SB_HEADS, SB_HEAD_DIM), sb_k_norm)
    vb = to_heads(sb_v, SB_HEADS, SB_HEAD_DIM)
    o_b = stick_breaking_attention(qb, kb, vb).transpose(0, 2, 1, 3).reshape(b, t, SB_WIDTH)
    y_b = o_b @ w_branch_b
    merged = jax.nn.sigmoid(gate_a) * y_a + jax.nn.sigmoid(gate_b) * y_b
    return merged @ w_out

def first_inputs(seed: int = 0) -> dict:
    key = jax.random.key(seed)
    ks = jax.random.split(key, 20)
    L = DEPTH

    def dense(k, shape, fan_in):
        return jax.random.normal(k, shape, jnp.float32) * (fan_in ** -0.5)

    def gain(k, shape):
        return 1.0 + 0.1 * jax.random.normal(k, shape, jnp.float32)

    dt = jnp.exp(jax.random.uniform(ks[8], (L, DN_HEADS), jnp.float32, math.log(1e-3), math.log(1e-1)))
    return {
        "x": jax.random.normal(ks[0], (BATCH, SEQ, D_MODEL), jnp.float32),
        "ffn1_norm": gain(ks[1], (L, D_MODEL)),
        "ffn1_w_in": dense(ks[2], (L, D_MODEL, 2 * D_FF), D_MODEL),
        "ffn1_w_out": dense(ks[3], (L, D_FF, D_MODEL), D_FF),
        "mix_norm": gain(ks[4], (L, D_MODEL)),
        "w_in": dense(ks[5], (L, D_MODEL, N_IN), D_MODEL),
        "dn_conv_w": dense(ks[6], (L, DN_CONV, 3 * DN_WIDTH), DN_CONV),
        "dn_a_log": jnp.log(jax.random.uniform(ks[7], (L, DN_HEADS), jnp.float32, 1.0, 16.0)),
        "dn_dt_bias": dt + jnp.log(-jnp.expm1(-dt)),
        "dn_out_norm": gain(ks[9], (L, DN_HEAD_DIM)),
        "sb_q_norm": gain(ks[10], (L, SB_HEAD_DIM)),
        "sb_k_norm": gain(ks[11], (L, SB_HEAD_DIM)),
        "w_branch_a": dense(ks[12], (L, DN_WIDTH, D_MODEL), DN_WIDTH),
        "w_branch_b": dense(ks[13], (L, SB_WIDTH, D_MODEL), SB_WIDTH),
        "w_out": dense(ks[14], (L, D_MODEL, D_MODEL), D_MODEL),
        "ffn2_norm": gain(ks[15], (L, D_MODEL)),
        "ffn2_w_in": dense(ks[16], (L, D_MODEL, 2 * D_FF), D_MODEL),
        "ffn2_w_out": dense(ks[17], (L, D_FF, D_MODEL), D_FF),
    }

def first_block(x, ffn1_norm, ffn1_w_in, ffn1_w_out, mix_norm, w_in, dn_conv_w, dn_a_log, dn_dt_bias,
              dn_out_norm, sb_q_norm, sb_k_norm, w_branch_a, w_branch_b, w_out,
              ffn2_norm, ffn2_w_in, ffn2_w_out):
    for l in range(DEPTH):
        x = x + FFN_HALF * swiglu(rmsnorm(x, ffn1_norm[l]), ffn1_w_in[l], ffn1_w_out[l])
        x = x + hybrid_mixer(rmsnorm(x, mix_norm[l]), w_in[l], dn_conv_w[l], dn_a_log[l], dn_dt_bias[l],
                             dn_out_norm[l], sb_q_norm[l], sb_k_norm[l],
                             w_branch_a[l], w_branch_b[l], w_out[l])
        x = x + FFN_HALF * swiglu(rmsnorm(x, ffn2_norm[l]), ffn2_w_in[l], ffn2_w_out[l])
    return x


CHUNK = 64
Q_BLOCK = 128
HEAD_DIM = 64
NORM_EPS = 1e-6

A_HEADS = 4
A_W = A_HEADS * HEAD_DIM
A_LEFT_CHUNKS = 8
A_MAX_REL = 128

B_HEADS = 4
B_Q_LORA = 256
B_KV_LORA = 128
B_NOPE = 64
B_ROPE = 32
B_V = 64
ROPE_THETA = 10000.0

C_HEADS = 4
C_W = C_HEADS * HEAD_DIM
FORGET_BIAS_MEAN = 3.0

CONV_CH = 256
CONV_K = 31

N_BRANCH = 4
BRANCH_W = 256
D_FF_2 = 4 * D_MODEL

IN_SPLITS = (A_W, A_W, A_W,
             B_Q_LORA, B_KV_LORA, B_ROPE,
             C_W, C_W, C_W, C_HEADS,
             CONV_CH, CONV_CH)
IN_COLS = sum(IN_SPLITS)


def _normal(key, shape, scale):
    return scale * jax.random.normal(key, shape, jnp.float32)

def rms_norm(x, g):
    xf = x.astype(jnp.float32)
    y = xf * lax.rsqrt(jnp.mean(xf * xf, axis=-1, keepdims=True) + NORM_EPS)
    return (y * g.astype(jnp.float32)).astype(x.dtype)

def layer_norm(x, g, b):
    xf = x.astype(jnp.float32)
    mu = jnp.mean(xf, axis=-1, keepdims=True)
    xc = xf - mu
    var = jnp.mean(xc * xc, axis=-1, keepdims=True)
    y = xc * lax.rsqrt(var + NORM_EPS) * g.astype(jnp.float32) + b.astype(jnp.float32)
    return y.astype(x.dtype)

def apply_rope(x, positions):
    half = x.shape[-1] // 2
    inv_freq = 1.0 / (ROPE_THETA ** (jnp.arange(half, dtype=jnp.float32) / half))
    ang = positions.astype(jnp.float32)[..., None] * inv_freq
    if x.ndim == 4:
        ang = ang[:, :, None, :]
    cos, sin = jnp.cos(ang), jnp.sin(ang)
    xf = x.astype(jnp.float32)
    x1, x2 = xf[..., :half], xf[..., half:]
    return jnp.concatenate([x1 * cos - x2 * sin, x2 * cos + x1 * sin], axis=-1).astype(x.dtype)

def chunk_band_attention(q, k, v, rel_table):
    b, s, h, d = q.shape
    nc = s // CHUNK
    w = A_LEFT_CHUNKS + 1
    qc = q.reshape(b, nc, CHUNK, h, d)

    def band(t):
        tc = t.reshape(b, nc, CHUNK, h, t.shape[-1])
        tp = jnp.pad(tc, ((0, 0), (A_LEFT_CHUNKS, 0), (0, 0), (0, 0), (0, 0)))
        return jnp.concatenate([tp[:, j:j + nc] for j in range(w)], axis=2)

    kb, vb = band(k), band(v)
    key_chunk = jnp.arange(nc)[:, None] + jnp.arange(w)[None, :] - A_LEFT_CHUNKS
    valid = jnp.repeat(key_chunk >= 0, CHUNK, axis=1)
    rel = (jnp.arange(CHUNK)[:, None] + A_LEFT_CHUNKS * CHUNK) - jnp.arange(w * CHUNK)[None, :]
    rel_idx = jnp.clip(rel, -A_MAX_REL, A_MAX_REL) + A_MAX_REL
    bias = rel_table[:, rel_idx].astype(jnp.float32)
    scores = jnp.einsum('bcqhd,bckhd->bchqk', qc, kb).astype(jnp.float32) * (d ** -0.5)
    scores = scores + bias[None, None]
    scores = jnp.where(valid[None, :, None, None, :], scores, -jnp.inf)
    p = jax.nn.softmax(scores, axis=-1).astype(v.dtype)
    out = jnp.einsum('bchqk,bckhd->bcqhd', p, vb)
    return out.reshape(b, s, h, -1)

def block_causal_attention(q, k, v, causal_unit, log_forget_cum=None):
    b, s, h, dk = q.shape
    nb = s // Q_BLOCK
    scale = dk ** -0.5
    key_unit = jnp.arange(s) // causal_unit
    qb = q.reshape(b, nb, Q_BLOCK, h, dk).swapaxes(0, 1)
    starts = jnp.arange(nb) * Q_BLOCK

    def attend(q_blk, start, f_blk):
        sc = jnp.einsum('bqhd,bkhd->bhqk', q_blk, k).astype(jnp.float32) * scale
        if f_blk is not None:
            f_k = log_forget_cum.transpose(0, 2, 1)[:, :, None, :]
            sc = sc + f_blk.transpose(0, 2, 1)[..., None] - f_k
        q_unit = (start + jnp.arange(Q_BLOCK)) // causal_unit
        mask = key_unit[None, :] <= q_unit[:, None]
        sc = jnp.where(mask[None, None], sc, -jnp.inf)
        p = jax.nn.softmax(sc, axis=-1).astype(v.dtype)
        return jnp.einsum('bhqk,bkhd->bqhd', p, v)

    if log_forget_cum is None:
        out = lax.map(lambda xs: attend(xs[0], xs[1], None), (qb, starts))
    else:
        fb = log_forget_cum.reshape(b, nb, Q_BLOCK, h).swapaxes(0, 1)
        out = lax.map(lambda xs: attend(xs[0], xs[1], xs[2]), (qb, starts, fb))
    return out.swapaxes(0, 1).reshape(b, s, h, -1)

def hybrid_layer(x, positions, g_mix, w_in, w_gate, b_gate, rel_bias, g_q_lat, w_uq, g_kv_lat, w_ukv,
                 b_forget, w_dw, b_dw, g_conv_ln, b_conv_ln, w_branch, w_o, g_ffn, w_up, w_down):
    b, s, _ = x.shape
    h = rms_norm(x, g_mix)
    split_points = [int(i) for i in np.cumsum(IN_SPLITS)[:-1]]
    (a_q, a_k, a_v, b_qlat, b_kvlat, b_krope,
     c_q, c_k, c_v, c_f, d_val, d_gate) = jnp.split(h @ w_in, split_points, axis=-1)

    def heads(t, n):
        return t.reshape(b, s, n, -1)

    out_a = chunk_band_attention(heads(a_q, A_HEADS), heads(a_k, A_HEADS), heads(a_v, A_HEADS), rel_bias)

    q = (rms_norm(b_qlat, g_q_lat) @ w_uq).reshape(b, s, B_HEADS, B_NOPE + B_ROPE)
    q = jnp.concatenate([q[..., :B_NOPE], apply_rope(q[..., B_NOPE:], positions)], axis=-1)
    kv = (rms_norm(b_kvlat, g_kv_lat) @ w_ukv).reshape(b, s, B_HEADS, B_NOPE + B_V)
    k_rot = apply_rope(b_krope, positions)
    k = jnp.concatenate([kv[..., :B_NOPE],
                         jnp.broadcast_to(k_rot[:, :, None, :], (b, s, B_HEADS, B_ROPE))], axis=-1)
    out_b = block_causal_attention(q, k, kv[..., B_NOPE:], CHUNK)

    log_f = jax.nn.log_sigmoid(c_f.astype(jnp.float32) + b_forget.astype(jnp.float32))
    f_cum = jnp.cumsum(log_f, axis=1)
    out_c = block_causal_attention(heads(c_q, C_HEADS), heads(c_k, C_HEADS), heads(c_v, C_HEADS), 1, f_cum)

    u = d_val * jax.nn.sigmoid(d_gate)
    u = lax.conv_general_dilated(u, w_dw[:, None, :], window_strides=(1,), padding=[(CONV_K - 1, 0)],
                                 dimension_numbers=('NWC', 'WIO', 'NWC'),
                                 feature_group_count=CONV_CH) + b_dw
    out_d = jax.nn.silu(layer_norm(u, g_conv_ln, b_conv_ln))

    branches = jnp.stack([out_a.reshape(b, s, BRANCH_W), out_b.reshape(b, s, BRANCH_W),
                          out_c.reshape(b, s, BRANCH_W), out_d], axis=2)
    proj = jnp.einsum('bsnc,ncd->bsnd', branches, w_branch)
    gates = jax.nn.sigmoid(h @ w_gate + b_gate).reshape(b, s, N_BRANCH, D_MODEL)
    x = x + jnp.sum(gates * proj, axis=2) @ w_o

    hf = rms_norm(x, g_ffn)
    x = x + jnp.square(jax.nn.relu(hf @ w_up)) @ w_down
    return x

def second_inputs(seed: int = 0) -> dict:
    key = jax.random.key(seed)
    ks = jax.random.split(key, 24)
    L = DEPTH
    x = _normal(ks[0], (BATCH, SEQ, D_MODEL), 1.0)
    offset = jax.random.randint(ks[1], (BATCH, 1), 0, 4 * SEQ, dtype=jnp.int32)
    positions = offset + jnp.arange(SEQ, dtype=jnp.int32)[None, :]
    return dict(
        x=x,
        positions=positions,
        g_mix=1.0 + _normal(ks[2], (L, D_MODEL), 0.05),
        w_in=_normal(ks[3], (L, D_MODEL, IN_COLS), D_MODEL ** -0.5),
        w_gate=_normal(ks[4], (L, D_MODEL, N_BRANCH * D_MODEL), D_MODEL ** -0.5),
        b_gate=_normal(ks[5], (L, N_BRANCH * D_MODEL), 0.02),
        rel_bias=_normal(ks[6], (L, A_HEADS, 2 * A_MAX_REL + 1), 0.2),
        g_q_lat=1.0 + _normal(ks[7], (L, B_Q_LORA), 0.05),
        w_uq=_normal(ks[8], (L, B_Q_LORA, B_HEADS * (B_NOPE + B_ROPE)), B_Q_LORA ** -0.5),
        g_kv_lat=1.0 + _normal(ks[9], (L, B_KV_LORA), 0.05),
        w_ukv=_normal(ks[10], (L, B_KV_LORA, B_HEADS * (B_NOPE + B_V)), B_KV_LORA ** -0.5),
        b_forget=FORGET_BIAS_MEAN + _normal(ks[11], (L, C_HEADS), 0.5),
        w_dw=_normal(ks[12], (L, CONV_K, CONV_CH), CONV_K ** -0.5),
        b_dw=_normal(ks[13], (L, CONV_CH), 0.02),
        g_conv_ln=1.0 + _normal(ks[14], (L, CONV_CH), 0.05),
        b_conv_ln=_normal(ks[15], (L, CONV_CH), 0.02),
        w_branch=_normal(ks[16], (L, N_BRANCH, BRANCH_W, D_MODEL), BRANCH_W ** -0.5),
        w_o=_normal(ks[17], (L, D_MODEL, D_MODEL), D_MODEL ** -0.5),
        g_ffn=1.0 + _normal(ks[18], (L, D_MODEL), 0.05),
        w_up=_normal(ks[19], (L, D_MODEL, D_FF_2), D_MODEL ** -0.5),
        w_down=_normal(ks[20], (L, D_FF_2, D_MODEL), D_FF_2 ** -0.5),
        g_final=1.0 + _normal(ks[21], (D_MODEL,), 0.05),
    )

def second_block(x, positions, g_mix, w_in, w_gate, b_gate, rel_bias, g_q_lat, w_uq, g_kv_lat, w_ukv,
              b_forget, w_dw, b_dw, g_conv_ln, b_conv_ln, w_branch, w_o, g_ffn, w_up, w_down, g_final):
    for l in range(DEPTH):
        x = hybrid_layer(x, positions, g_mix[l], w_in[l], w_gate[l], b_gate[l], rel_bias[l],
                         g_q_lat[l], w_uq[l], g_kv_lat[l], w_ukv[l], b_forget[l], w_dw[l], b_dw[l],
                         g_conv_ln[l], b_conv_ln[l], w_branch[l], w_o[l], g_ffn[l], w_up[l], w_down[l])
    return rms_norm(x, g_final)


def setup_inputs(seed=0):
    out = dict(first_inputs(seed))
    for name, value in second_inputs(seed + 1).items():
        if name != "x":
            out[name + "_2"] = value
    return out


def reference(
    x, ffn1_norm, ffn1_w_in, ffn1_w_out, mix_norm, w_in, dn_conv_w, dn_a_log, dn_dt_bias,
    dn_out_norm, sb_q_norm, sb_k_norm, w_branch_a, w_branch_b, w_out, ffn2_norm, ffn2_w_in,
    ffn2_w_out, positions_2, g_mix_2, w_in_2, w_gate_2, b_gate_2, rel_bias_2, g_q_lat_2, w_uq_2,
    g_kv_lat_2, w_ukv_2, b_forget_2, w_dw_2, b_dw_2, g_conv_ln_2, b_conv_ln_2, w_branch_2,
    w_o_2, g_ffn_2, w_up_2, w_down_2, g_final_2,
):
    x = first_block(
        x, ffn1_norm, ffn1_w_in, ffn1_w_out, mix_norm, w_in, dn_conv_w, dn_a_log, dn_dt_bias,
        dn_out_norm, sb_q_norm, sb_k_norm, w_branch_a, w_branch_b, w_out, ffn2_norm, ffn2_w_in,
        ffn2_w_out,
    )
    return second_block(
        x, positions_2, g_mix_2, w_in_2, w_gate_2, b_gate_2, rel_bias_2, g_q_lat_2, w_uq_2,
        g_kv_lat_2, w_ukv_2, b_forget_2, w_dw_2, b_dw_2, g_conv_ln_2, b_conv_ln_2, w_branch_2,
        w_o_2, g_ffn_2, w_up_2, w_down_2, g_final_2,
    )


_drawn_inputs = setup_inputs


def setup_inputs(seed=0):
    import zlib

    import numpy as np

    out = dict(_drawn_inputs(seed))
    spreads = {}
    factors = {'b_gate_2': 8.0,
     'rel_bias_2': 3.882,
     'g_q_lat_2': 8.0,
     'g_kv_lat_2': 7.959,
     'b_dw_2': 3.899,
     'g_conv_ln_2': 2.877,
     'b_conv_ln_2': 8.0}
    for name, (base, spread) in spreads.items():
        noise = np.random.default_rng([zlib.crc32(name.encode()), seed]).standard_normal(out[name].shape)
        drawn = base * np.exp(spread * noise) if base else spread * noise
        out[name] = __import__('jax').numpy.asarray(drawn.astype(out[name].dtype))
    for name, factor in factors.items():
        out[name] = (out[name] * factor).astype(out[name].dtype)
    return out
```

```python
import math
from contextlib import ExitStack

import concourse.bass as bass
from concourse import mybir

F32 = mybir.dt.float32
F32R = mybir.dt.float32r
I32 = mybir.dt.int32
ALU = mybir.AluOpType
ACT = mybir.ActivationFunctionType
AX = mybir.AxisListType

P = 128
D = 1024
T = 256
TT = T // P
KC = D // P
DEPTH = 2
EPS = 1e-6
UNIT = 2048
SLOTS = 3
FF1 = 2816
FF1_BLOCKS = FF1 // 256
FF2 = 4096
FF2_BLOCKS = FF2 // 256
U_FFN1 = 3 * FF1_BLOCKS
U_MIX1 = 48
U_MIX2 = 34
U_FFN2 = 2 * FF2_BLOCKS
ROUNDS_1 = (2 * U_FFN1 + U_MIX1) // SLOTS
ROUNDS_2 = (U_MIX2 + U_FFN2) // SLOTS
SUB_1, SUB_2 = 3, 2
ARENA = 19712
HEADS = 8
GROUPS = HEADS // 2
ROUNDER = 1.5 * 2.0 ** 23
TURN = (6.28125, 0.001934051513671875, 1.255665914356996e-06)
PI = 3.1415925
MASKED = -1e30
LEVELS = 7


class Event:

    def __init__(self, sem, per, start=0):
        self.sem, self.per, self.start = sem, per, start

    def __call__(self, layer, step=0):
        return self.sem, layer * self.per + (self.start + step + 1)

    def reused(self, per):
        return Event(self.sem, per, DEPTH * self.per + self.start)


def constants():
    import numpy as np
    i = np.arange(P)
    r, c = i[:, None], i[None, :]
    parts = {"ident": r == c, "ones": np.ones((P, P)), "le": r <= c, "ge": r >= c}
    for s in range(LEVELS):
        parts[f"level{s}"] = (r >> (s + 1) == c >> (s + 1)) & (r >> s & 1 == 1) & (c >> s & 1 == 0)
    at, where = 0, {}
    for name, a in parts.items():
        where[name] = (at, at + a.shape[1])
        at += a.shape[1]
    return where, np.concatenate([a.astype(np.float32) for a in parts.values()], axis=1)


def constants_2():
    import numpy as np
    i = np.arange(P)
    r, c = i[:, None], i[None, :]
    half = np.arange(16, dtype=np.float32)
    inv_freq = (np.float32(1.0) / np.power(np.float32(10000.0), half / np.float32(16.0))).astype(np.float32)
    turn = np.zeros((P, 96), np.float32)
    for n in range(64, 80):
        turn[n + 16, n] = -1.0
        turn[n, n + 16] = 1.0
    freq = np.zeros((P, 1), np.float32)
    freq[64:96, 0] = np.tile(inv_freq, 2)
    parts = {"ones2": np.ones((P, T)), "minus": -np.ones((P, P)),
             "chunk": np.where(r // 64 > c // 64, MASKED, 0.0), "causal": np.where(r > c, MASKED, 0.0),
             "turn": turn, "freq": freq}
    at, where = 0, {}
    for name, a in parts.items():
        where[name] = (at, at + a.shape[1])
        at += a.shape[1]
    return where, np.concatenate([a.astype(np.float32) for a in parts.values()], axis=1)


CONST_AT, CONSTANTS = constants()
CONST2_AT, CONSTANTS2 = constants_2()


def hybrid_stack_kernel(nc, d, out):
    ctx = ExitStack()
    with ctx:
        def sb(name, shape, dt=F32):
            return ctx.enter_context(nc.sbuf_tensor(name, shape, dt))

        def sem(name):
            return ctx.enter_context(nc.semaphore(name))

        bank = [ctx.enter_context(nc.psum_tensor(f"bank{i}", [P, 512], F32)) for i in range(8)]
        raw = [sb(f"raw{s}", [P, UNIT]) for s in range(SLOTS)]
        whi = [sb(f"whi{s}", [P, UNIT], F32R) for s in range(SLOTS)]
        wlo = [sb(f"wlo{s}", [P, UNIT], F32R) for s in range(SLOTS)]
        x = sb("x", [P, TT, D])
        xhi = sb("xhi", [P, KC, T], F32R)
        xlo = sb("xlo", [P, KC, T], F32R)
        yhi = sb("yhi", [P, KC, T], F32R)
        ylo = sb("ylo", [P, KC, T], F32R)
        zero = sb("zero", [P, 512], F32R)
        table = sb("table", [P, CONSTANTS.shape[1]])

        def const(name):
            a, b = CONST_AT[name]
            return table[:, a:b]

        ident, ones, le, ge = const("ident"), const("ones"), const("le"), const("ge")
        const_cols = sb("const_cols", [P, 4])
        eps, one, ln_scale, half_pi = [const_cols[:, i:i + 1] for i in range(4)]
        NV = 104
        cols = sb("cols", [P, NV])
        conv_w = sb("conv_w", [P, DEPTH * 96])
        dt_bias = sb("dt_bias", [P, DEPTH * HEADS])
        a_log = sb("a_log", [P, DEPTH * HEADS])
        sumsq = sb("sumsq", [P, TT])
        lnv = sb("lnv", [P, TT])
        rstd = sb("rstd", [P, TT])
        arena = sb("arena", [P, ARENA])
        gate_bias = sb("gate_bias", [P, DEPTH * 32])
        dw = sb("dw", [P, DEPTH * 62])
        b_forget = sb("b_forget", [P, DEPTH * 4])
        rotary = sb("rotary", [96, 2 * T])
        rows = arena[:, 4096:4224]
        gate_rows = arena[0:DEPTH * 32, 4608:4736]
        dw_rows = arena[0:DEPTH * 62, 4736:4864]
        ext = arena[0:DEPTH * 4, 4864:5248]
        positions = arena[64:96, 5248:5504].bitcast(I32)
        angle, turns, angle_tmp = [arena[64:96, 5504 + i * 256:5760 + i * 256] for i in range(3)]
        bias_rows = nc.dram_tensor("bias_rows", [DEPTH, 4, P, 384], F32, kind="Internal").ap()
        conv_rows = arena[0:96, 4352:4608].rearrange("p (l n) -> p l n", l=DEPTH)
        pre = [sb(f"pre{i}", [P, 2, T + 3]) for i in range(2)]
        small = sb("small", [P, 256])
        ba_w = (sb("ba_raw", [P, KC, 16]), sb("ba_hi", [P, KC, 16], F32R), sb("ba_lo", [P, KC, 16], F32R))
        xn = arena[:, 0:TT * D].rearrange("p (t d) -> p t d", t=TT)
        eg = arena[:, 2048:2560]
        hbuf = arena[:, 2560:3072]
        hhi = yhi[:, 0:2, :]
        hlo = ylo[:, 0:2, :]

        def as_in(w):
            return w[:].rearrange("p (c n) -> p c n", c=KC)

        def as_out(w):
            return w[:].rearrange("p (c n) -> p c n", c=2)

        tp = [bank[4 + b][:].rearrange("p (c t) -> p c t", c=2) for b in range(4)]

        raw_in = [sem(f"raw_in{s}") for s in range(SLOTS)]
        hi_done = [sem(f"hi_done{s}") for s in range(SLOTS)]
        lo_done = [sem(f"lo_done{s}") for s in range(SLOTS)]
        multiplied = [sem(f"multiplied{s}") for s in range(SLOTS)]
        loaded = sem("loaded")
        consts = sem("consts")
        cols_t = sem("cols_t")
        cols_done = sem("cols_done")
        x_new = [sem(f"x_new{t}") for t in range(TT)]
        sumsq_done = sem("sumsq_done")
        ln_done = sem("ln_done")
        rstd_done = sem("rstd_done")
        xn_done = sem("xn_done")
        xt_done = sem("xt_done")
        xhi_done = sem("xhi_done")
        xlo_done = sem("xlo_done")
        exp_gate = sem("exp_gate")
        gated = sem("gated")
        abs_gate = sem("abs_gate")
        ln_gate = sem("ln_gate")
        log_sigmoid = sem("log_sigmoid")
        sigmoid_gate = sem("sigmoid_gate")
        h_done = sem("h_done")
        hhi_done = sem("hhi_done")
        hlo_done = sem("hlo_done")
        stored = sem("stored")
        table2_in = sem("table2_in")
        ext_done = sem("ext_done")
        angle_step = sem("angle_step")
        rotary_step = sem("rotary_step")
        final_done = sem("final_done")
        pool_waited = sem("pool_waited")
        sync_waited = sem("sync_waited")

        COL = {}
        at = 0
        for name, per in (("ffn1_norm", 8), ("mix_norm", 8), ("ffn2_norm", 8), ("g_mix_2", 8), ("g_ffn_2", 8),
                          ("dn_out_norm", 1), ("sb_q_norm", 1), ("sb_k_norm", 1), ("g_q_lat_2", 2),
                          ("g_kv_lat_2", 1), ("b_dw_2", 2), ("g_conv_ln_2", 2), ("b_conv_ln_2", 2)):
            COL[name] = (at, per)
            at += DEPTH * per
        assert at == NV

        def col(name, l, c=0):
            a, per = COL[name]
            i = l * per + (a + c)
            return cols[:, bass.ds(i, 1)] if not isinstance(i, int) else cols[:, i:i + 1]

        def unit(r0, u, i=0):
            return u % SLOTS, r0 + (u // SLOTS) + i

        def load_unit(e, n, src, view, first=False):
            s, r = n
            e.wait_ge(lo_done[s], r)
            if first:
                e.sem_inc(sync_waited)
            e.dma_start(view(raw[s]), src).then_inc(raw_in[s], 16)

        def split_hi(e, n):
            s, r = n
            e.wait_ge(raw_in[s], r * 16)
            e.wait_ge(multiplied[s], r)
            e.activation(whi[s][:], raw[s][:], ACT.Copy).then_inc(hi_done[s], 1)

        def split_lo(e, n):
            s, r = n
            e.wait_ge(hi_done[s], r)
            e.wait_ge(raw_in[s], r * 16)
            e.tensor_tensor(wlo[s][:], raw[s][:], whi[s][:].bitcast(F32), ALU.subtract).then_inc(lo_done[s], 1)

        def split_ready(e, n):
            s, r = n
            e.wait_ge(lo_done[s], r + 1)

        def product3(e, o, ahi, alo, bhi, blo, start, stop):
            e.matmul(o, ahi, bhi, start=start, stop=False, skip_group_check=True)
            e.matmul(o, ahi, blo, start=False, stop=False, skip_group_check=True)
            return e.matmul(o, alo, bhi, start=False, stop=stop, skip_group_check=True)

        def feature_product(e, n, o, bhi, blo):
            s, _ = n
            split_ready(e, n)
            for b in range(2):
                for c in range(KC):
                    mm = product3(e, o[:, b * T:(b + 1) * T], as_in(whi[s])[:, c, b * P:(b + 1) * P],
                                  as_in(wlo[s])[:, c, b * P:(b + 1) * P], bhi[:, c, :], blo[:, c, :],
                                  c == 0, c == KC - 1)
            mm.then_inc(multiplied[s], 1)

        def row_product(e, n, ahi, alo, stop):
            s, _ = n
            split_ready(e, n)
            for t in range(TT):
                for h in range(2):
                    for c in range(2):
                        mm = product3(e, bank[2 * t + h][:], ahi[:, c, t * P:(t + 1) * P], alo[:, c, t * P:(t + 1) * P],
                                      as_out(whi[s])[:, c, h * 512:(h + 1) * 512],
                                      as_out(wlo[s])[:, c, h * 512:(h + 1) * 512], False, stop and c == 1)
            mm.then_inc(multiplied[s], 1)

        def clear_rows(e):
            for b in range(4):
                e.matmul(bank[b][:], zero[:, 0:P], zero[:], start=True, stop=False, skip_group_check=True)

        def add_rows(e, n, scale):
            s, r = n
            e.wait_ge(multiplied[s], r + 1)
            for t in range(TT):
                for h in range(2):
                    part = x[:, t, h * 512:(h + 1) * 512]
                    up = e.scalar_tensor_tensor(part, bank[2 * t + h][:], scale, part, ALU.mult, ALU.add)
                up.then_inc(x_new[t], 1)

        def rstd_act(e, j):
            for t in range(TT):
                e.wait_ge(x_new[t], 1 + j)
                e.activation(xn[:, t, :], x[:, t, :], ACT.Square, accum_out=sumsq[:, t:t + 1]).then_inc(sumsq_done, 1)
                e.wait_ge(sumsq_done, j * TT + (t + 1))
                e.activation(lnv[:, t:t + 1], sumsq[:, t:t + 1], ACT.Ln, bias=eps, scale=1.0 / D).then_inc(ln_done, 1)
                e.wait_ge(ln_done, j * TT + (t + 1))
                e.activation(rstd[:, t:t + 1], lnv[:, t:t + 1], ACT.Exp, scale=-0.5).then_inc(rstd_done, 1)

        def norm_act(e, j, gain):
            rstd_act(e, j)
            for c in range(KC):
                e.wait_ge(xt_done, j * 4 + (c // 2 + 1))
                e.activation(xhi[:, c, :], tp[c // 2][:, c % 2, :], ACT.Copy, scale=gain(c)).then_inc(xhi_done, 1)

        def scale_dve(e, j):
            for t in range(TT):
                e.wait_ge(rstd_done, j * TT + (t + 1))
                e.tensor_scalar(xn[:, t, :], x[:, t, :], rstd[:, t:t + 1], None, ALU.mult).then_inc(xn_done, 1)

        def norm_dve(e, j, gain):
            scale_dve(e, j)
            for c in range(KC):
                e.wait_ge(xhi_done, j * KC + (c // 2 * 2 + 2))
                e.scalar_tensor_tensor(xlo[:, c, :], tp[c // 2][:, c % 2, :], gain(c), xhi[:, c, :].bitcast(F32),
                                       ALU.mult, ALU.subtract).then_inc(xlo_done, 1)

        def norm_pe(e, j):
            for t in range(TT):
                e.wait_ge(xn_done, j * TT + (t + 1))
                for c in range(KC):
                    mm = e.transpose(tp[c // 2][:, c % 2, t * P:(t + 1) * P], xn[:, t, c * P:(c + 1) * P], ident)
                    if t == TT - 1 and c % 2:
                        mm.then_inc(xt_done, 1)
            clear_rows(e)

        def norm_ready(e, j):
            e.wait_ge(xhi_done, j * KC + KC)
            e.wait_ge(xlo_done, j * KC + KC)

        GATE, UP = bank[4], bank[5]

        def ffn1_sync(e, l, r0, u0, w_in, w_down):
            def cols_of(i, first):
                return w_in[l, :, bass.ds(i * 256 + first, 256)].rearrange("(c p) n -> p c n", p=P)

            def rows_of(i):
                return w_down[l, bass.ds(i * 256, 256), :].rearrange("(c p) n -> p c n", p=P)

            load_unit(e, unit(r0, u0), w_in[l, :, 0:256].rearrange("(c p) n -> p c n", p=P), as_in)
            load_unit(e, unit(r0, u0 + 1), w_in[l, :, FF1:FF1 + 256].rearrange("(c p) n -> p c n", p=P), as_in)
            with e.Fori(1, FF1_BLOCKS) as i:
                load_unit(e, unit(r0 - 1, u0 + 2, i), cols_of(i, 0), as_in)
                load_unit(e, unit(r0 - 1, u0 + 3, i), cols_of(i, FF1), as_in)
                load_unit(e, unit(r0 - 1, u0 + 4, i), rows_of(i - 1), as_out)
            load_unit(e, unit(r0, u0 + 32), w_down[l, FF1 - 256:FF1, :].rearrange("(c p) n -> p c n", p=P), as_out)

        def ffn1_pe(e, l, r0, u0, j, f):
            norm_pe(e, j)
            norm_ready(e, j)
            def gate_up(ug, uu, i):
                e.wait_ge(h_done, 1 + f * FF1_BLOCKS + i)
                feature_product(e, ug, GATE, xhi, xlo)
                feature_product(e, uu, UP, xhi, xlo)

            def down(u, i, stop):
                e.wait_ge(hhi_done, f * FF1_BLOCKS + i + 1)
                e.wait_ge(hlo_done, 1 + f * FF1_BLOCKS + i + 1)
                row_product(e, u, hhi, hlo, stop)

            gate_up(unit(r0, u0), unit(r0, u0 + 1), 0)
            with e.Fori(1, FF1_BLOCKS) as i:
                gate_up(unit(r0 - 1, u0 + 2, i), unit(r0 - 1, u0 + 3, i), i)
                down(unit(r0 - 1, u0 + 4, i), i - 1, False)
            down(unit(r0, u0 + 32), FF1_BLOCKS - 1, True)

        def ffn1_act(e, l, r0, u0, j, f, gain):
            split_hi(e, unit(r0, u0))
            split_hi(e, unit(r0, u0 + 1))
            norm_act(e, j, gain)

            def exp_of_gate(u, i):
                n = f * FF1_BLOCKS + i
                e.wait_ge(multiplied[u[0]], u[1] + 1)
                e.wait_ge(gated, 1 + n)
                e.activation(eg, GATE[:], ACT.Abs).then_inc(abs_gate, 1)
                e.wait_ge(abs_gate, n + 1)
                e.activation(eg, eg, ACT.Exp, scale=-1.0).then_inc(exp_gate, 1)
                e.wait_ge(exp_gate, n + 1)
                e.activation(eg, eg, ACT.Ln, bias=one).then_inc(ln_gate, 1)

            def sigmoid_of_gate(i):
                n = f * FF1_BLOCKS + i
                e.wait_ge(log_sigmoid, n + 1)
                e.activation(eg, eg, ACT.Exp).then_inc(sigmoid_gate, 1)

            def split_h(last_down, i):
                e.wait_ge(h_done, 1 + f * FF1_BLOCKS + i + 1)
                if last_down is not None:
                    e.wait_ge(multiplied[last_down[0]], last_down[1] + 1)
                e.activation(hhi.rearrange("p c t -> p (c t)"), hbuf, ACT.Copy).then_inc(hhi_done, 1)

            split_hi(e, unit(r0, u0 + 2))
            exp_of_gate(unit(r0, u0), 0)
            split_hi(e, unit(r0, u0 + 3))
            sigmoid_of_gate(0)
            split_h(None, 0)
            with e.Fori(1, FF1_BLOCKS - 1) as i:
                split_hi(e, unit(r0 - 1, u0 + 4, i))
                exp_of_gate(unit(r0 - 1, u0 + 2, i), i)
                split_hi(e, unit(r0 - 1, u0 + 5, i))
                sigmoid_of_gate(i)
                split_hi(e, unit(r0 - 1, u0 + 6, i))
                split_h(unit(r0 - 1, u0 + 4, i), i)
            i = FF1_BLOCKS - 1
            split_hi(e, unit(r0, u0 + 31))
            exp_of_gate(unit(r0, u0 + 29), i)
            split_hi(e, unit(r0, u0 + 32))
            sigmoid_of_gate(i)
            split_h(unit(r0, u0 + 31), i)

        def ffn1_dve(e, l, r0, u0, j, f, gain):
            split_lo(e, unit(r0, u0))
            split_lo(e, unit(r0, u0 + 1))
            norm_dve(e, j, gain)

            def log_sigmoid_of_gate(i):
                n = f * FF1_BLOCKS + i
                e.wait_ge(ln_gate, n + 1)
                e.scalar_tensor_tensor(eg, GATE[:], 0.0, eg, ALU.min, ALU.subtract).then_inc(log_sigmoid, 1)

            def gate_h(uu, i):
                n = f * FF1_BLOCKS + i
                e.wait_ge(sigmoid_gate, n + 1)
                e.wait_ge(hlo_done, 1 + n)
                e.tensor_tensor(hbuf, eg, GATE[:], ALU.mult).then_inc(gated, 1)
                e.wait_ge(gated, 1 + n + 1)
                e.wait_ge(multiplied[uu[0]], uu[1] + 1)
                e.tensor_tensor(hbuf, hbuf, UP[:], ALU.mult).then_inc(h_done, 1)

            def split_h(i):
                e.wait_ge(hhi_done, f * FF1_BLOCKS + i + 1)
                e.tensor_tensor(hlo.rearrange("p c t -> p (c t)"), hbuf, hhi.rearrange("p c t -> p (c t)").bitcast(F32),
                                ALU.subtract).then_inc(hlo_done, 1)

            split_lo(e, unit(r0, u0 + 2))
            log_sigmoid_of_gate(0)
            split_lo(e, unit(r0, u0 + 3))
            gate_h(unit(r0, u0 + 1), 0)
            split_h(0)
            with e.Fori(1, FF1_BLOCKS - 1) as i:
                split_lo(e, unit(r0 - 1, u0 + 4, i))
                log_sigmoid_of_gate(i)
                split_lo(e, unit(r0 - 1, u0 + 5, i))
                gate_h(unit(r0 - 1, u0 + 3, i), i)
                split_lo(e, unit(r0 - 1, u0 + 6, i))
                split_h(i)
            i = FF1_BLOCKS - 1
            split_lo(e, unit(r0, u0 + 31))
            log_sigmoid_of_gate(i)
            split_lo(e, unit(r0, u0 + 32))
            gate_h(unit(r0, u0 + 30), i)
            split_h(i)
            add_rows(e, unit(r0, u0 + 32), 0.5)

        KINDS = ("q", "k", "v", "sq", "sk", "sv", "z")
        KIND_COL = (0, D, 2 * D, 4 * D + 16, 5 * D + 16, 6 * D + 16, 3 * D)
        GATE_A_COL, GATE_B_COL = 7 * D + 16, 8 * D + 16
        BA_COL = 4 * D
        N1 = 28
        PAIRS = 8
        feat = [arena[:, k * 2048:(k + 1) * 2048].rearrange("p (h t) -> p h t", t=T) for k in (0, 1, 2, 4, 5)]
        qT, kT, vT, sqT, skT = feat
        zT = arena[:, 6144:8192].rearrange("p (h t) -> p h t", t=T)
        sv = arena[:, 12288:14336].rearrange("p (t n) -> p t n", t=TT)
        HOME = [qT, kT, vT, sqT, skT, None, zT]
        sg = [arena[:, 14336 + i * 512:14848 + i * 512] for i in range(2)]
        sqr = [arena[:, 15360 + i * 512:15872 + i * 512] for i in range(2)]
        rr = [arena[:, 16384 + i * 512:16896 + i * 512] for i in range(2)]
        att = [[arena[:, 17408 + (i * 3 + j) * 384:17792 + (i * 3 + j) * 384] for j in range(3)] for i in range(2)]

        def dbuf(g, j):
            a = 8192 + (g * 5 + j) * 512
            return arena[:, a:a + 512].rearrange("p (i n) -> p i n", i=4)

        Lb, Ub, Tb, Mb, Ab = [[dbuf(g, j) for g in range(GROUPS)] for j in range(5)]
        egb = [arena[:, 18464 + g * 256:18464 + (g + 1) * 256].rearrange("p (i n) -> p i n", i=2) for g in range(GROUPS)]
        merged = arena[:, 8192:10240].rearrange("p (c t) -> p c t", t=T)
        sgm = arena[:, 10240:10752]
        ytmp = arena[:, 10752:11264]
        ba, bt, bu, beta, gg, cum, ebg = [small[:, i * 32:(i + 1) * 32] for i in range(7)]
        ekd = small[:, 224:232]
        glast = small[:, 232:240]
        ba_raw, ba_hi, ba_lo = ba_w

        def ev(name, per):
            return Event(sem(name), per)

        ba_in = ev("ba_in", 1)
        V = {n: ev(n, p) for n, p in dict(
            ba_hi_done=1, ba_lo_done=1, ba_product=1, ba_kept=1, exp_b=1, one_b=1, beta_done=1, a_shift=1, abs_a=1,
            exp_a=1, ln_a=1, softplus_a=1, exp_alog=1, g_done=1, cum_product=1, cum_kept=1, exp_cum=1, ebg_done=1,
            pre_copied=12, tap=48, kept=16, s_abs=16, s_exp=16, s_ln=16, s_min=16, s_sigmoid=16, silu=16,
            squared=16, square_sum=16, ln_sum=16, rnorm=16, normed=16,
            z_product=8, z_kept=8, z_abs=8, z_exp=8, z_ln=8, softplus=8, sp_masked=8, r_product=8, z_minus=8,
            w_exp=8, w_masked=8, o_product=8, o_hi=8, o_lo=8,
            g_spread=4, g_rows=4, x_abs=4, glast_kept=4, ekd_done=4, egb_done=4, kk=4, qk=4, decay=4, a_mask=4, l_done=4,
            attn_done=4, m_ready=28, m_product=24, w_kept=24, tu_product=28, tu_done=28,
            kv_turned=4, k_scaled=4, v_scaled=4, uw_product=4, u_kept=4, w_copied=4, s_product=4, s_kept=4,
            ws_product=4, v_new=4, q_decayed=4, od_product=4, od_squared=4, od_sum=4, od_ln=4, od_r=4, od_norm=4,
            od_gated=4, oa_hi=4, oa_lo=4,
            p_abs=8, p_exp=8, p_ln=8, p_min=8, p_sigmoid=8, p_scaled=8, p_merged=8, m_hi=4, m_lo=4).items()}
        V["ba_lo_done"].start = 1

        def mix1_unit(r0, u0, n):
            return unit(r0, u0 + n)

        def mix1_sync(e, l, r0, u0):
            w = d["w_in"]

            def columns(w, c):
                return w[l, :, c:c + 256].rearrange("(c p) n -> p c n", p=P)

            e.wait_ge(V["ba_lo_done"].sem, 1 + l)
            e.dma_start(ba_raw[:], w[l, :, BA_COL:BA_COL + 16].rearrange("(c p) n -> p c n", p=P)).then_inc(ba_in.sem, 16)
            for n in range(N1):
                load_unit(e, unit(r0, u0 + n), columns(w, KIND_COL[n // 4] + n % 4 * 256), as_in, n == 0)
            for k, (gc, wb) in enumerate(((GATE_B_COL, d["w_branch_b"]), (GATE_A_COL, d["w_branch_a"]))):
                for g in range(4):
                    n = N1 + 8 * k + 2 * g
                    load_unit(e, unit(r0, u0 + n), columns(w, gc + g * 256), as_in)
                    load_unit(e, unit(r0, u0 + n + 1), columns(wb, g * 256), as_in)
            for g in range(4):
                load_unit(e, unit(r0, u0 + 44 + g),
                          d["w_out"][l, g * 256:(g + 1) * 256, :].rearrange("(c p) n -> p c n", p=P), as_out)

        def b4(i):
            return bank[i][:].rearrange("p (i n) -> p i n", i=4)

        def b2(i):
            return bank[i][:].rearrange("p (h t) -> p h t", h=2)

        def row_unit(e, n, o, ahi, alo):
            s, _ = n
            split_ready(e, n)
            for t in range(TT):
                for c in range(KC):
                    mm = product3(e, o[:, t * 256:(t + 1) * 256], ahi[:, c, t * P:(t + 1) * P], alo[:, c, t * P:(t + 1) * P],
                                  as_in(whi[s])[:, c, :], as_in(wlo[s])[:, c, :], c == 0, c == KC - 1)
            mm.then_inc(multiplied[s], 1)

        SILU = list(range(12)) + [24, 25, 26, 27]
        NORM = list(range(8)) + list(range(12, 20))

        def mix1_pe(e, l, r0, u0, j):
            norm_pe(e, j)
            norm_ready(e, j)
            e.wait_ge(*V["ba_hi_done"](l))
            e.wait_ge(*V["ba_lo_done"](l))
            for t in range(TT):
                for c in range(KC):
                    mm = product3(e, bank[2][:, t * 16:(t + 1) * 16], xhi[:, c, t * P:(t + 1) * P],
                                  xlo[:, c, t * P:(t + 1) * P], ba_hi[:, c, :], ba_lo[:, c, :], c == 0, c == KC - 1)
            mm.then_inc(V["ba_product"].sem, 1)
            for n in range(N1 + 2):
                if n < N1:
                    if n >= 2:
                        kept_unit(e, l, n - 2)
                    if n // 4 == 5:
                        row_unit(e, unit(r0, u0 + n), bank[n % 2], xhi, xlo)
                    else:
                        feature_product(e, unit(r0, u0 + n), bank[n % 2], xhi, xlo)
                if n == 1:
                    e.wait_ge(*V["g_done"](l))
                    e.matmul(bank[2][:, 0:16], le, gg[:, 0:16], start=True, stop=True).then_inc(V["cum_product"].sem, 1)
                if n - 2 in NORM:
                    m = NORM.index(n - 2)
                    e.wait_ge(*V["squared"](l, m))
                    if m >= 2:
                        e.wait_ge(*V["ln_sum"](l, m - 2))
                    if m == 0:
                        e.wait_ge(*V["cum_kept"](l))
                    e.matmul(bank[2 + m % 2][:], ones, sqr[m % 2], start=True, stop=True).then_inc(V["square_sum"].sem, 1)
            mix1_attention_pe(e, l)
            mix1_delta_pe(e, l)
            for n in range(PAIRS):
                gu, yu = unit(r0, u0 + N1 + 2 * n), unit(r0, u0 + N1 + 2 * n + 1)
                if n == 0:
                    e.wait_ge(*V["od_norm"](l, 1))
                else:
                    e.wait_ge(*V["p_scaled"](l, n - 1))
                feature_product(e, gu, bank[0], xhi, xlo)
                if n == 0:
                    e.wait_ge(*V["o_lo"](l, HEADS - 1))
                if n == 4:
                    e.wait_ge(*V["oa_lo"](l, GROUPS - 1))
                feature_product(e, yu, bank[1], yhi, ylo)
            e.wait_ge(*V["od_gated"](l, GROUPS - 1))
            clear_rows_from(e, l)
            for g in range(4):
                e.wait_ge(*V["m_lo"](l, g))
                row_product(e, unit(r0, u0 + 44 + g), xhi[:, 2 * g:2 * g + 2, :], xlo[:, 2 * g:2 * g + 2, :], g == 3)

        def clear_rows_from(e, l):
            e.wait_ge(*V["p_scaled"](l, PAIRS - 1))
            clear_rows(e)

        def kept_unit(e, l, n):
            if n < 12:
                e.wait_ge(*V["pre_copied"](l, n))
            else:
                e.wait_ge(*V["kept"](l, n - 12))

        def wait_unit(e, r0, u0, n):
            s, r = unit(r0, u0 + n)
            e.wait_ge(multiplied[s], r + 1)

        def home(n):
            k, g = n // 4, n % 4
            return HOME[k][:, 2 * g:2 * g + 2, :].rearrange("p h t -> p (h t)")

        def mix1_act(e, l, r0, u0, j):
            split_hi(e, unit(r0, u0))
            split_hi(e, unit(r0, u0 + 1))
            e.wait_ge(ba_in.sem, l * 16 + 16)
            e.wait_ge(multiplied[(u0 - 1) % SLOTS], r0 + (u0 - 1) // SLOTS + 1)
            e.activation(ba_hi[:], ba_raw[:], ACT.Copy).then_inc(V["ba_hi_done"].sem, 1)
            norm_act(e, j, lambda c: col("mix_norm", l, c))
            for n in range(N1 + 3):
                if n + 2 <= N1 + 2:
                    split_hi(e, unit(r0, u0 + n + 2))
                if n < N1:
                    wait_unit(e, r0, u0, n)
                    if n < 12:
                        if n >= 2:
                            e.wait_ge(*V["tap"](l, (n - 2) * 4 + 3))
                        e.activation(pre[n % 2][:, :, 3:3 + T], b2(n % 2), ACT.Copy).then_inc(V["pre_copied"].sem, 1)
                    elif n // 4 == 5:
                        g = n % 4
                        e.activation(sv[:, :, g * 256:(g + 1) * 256], b2(n % 2), ACT.Copy).then_inc(V["kept"].sem, 1)
                    else:
                        e.activation(home(n), bank[n % 2][:], ACT.Copy).then_inc(V["kept"].sem, 1)
                if n == 0:
                    small_act_1(e, l)
                if n == 1:
                    small_act_2(e, l)
                if n - 1 in SILU:
                    m = SILU.index(n - 1)
                    src = home(n - 1)
                    if m < 12:
                        e.wait_ge(*V["tap"](l, m * 4 + 3))
                    else:
                        e.wait_ge(*V["kept"](l, m))
                    if m >= 2:
                        e.wait_ge(*V["silu"](l, m - 2))
                    e.activation(sg[m % 2], src, ACT.Abs).then_inc(V["s_abs"].sem, 1)
                    e.wait_ge(*V["s_abs"](l, m))
                    e.activation(sg[m % 2], sg[m % 2], ACT.Exp, scale=-1.0).then_inc(V["s_exp"].sem, 1)
                    e.wait_ge(*V["s_exp"](l, m))
                    e.activation(sg[m % 2], sg[m % 2], ACT.Ln, bias=one).then_inc(V["s_ln"].sem, 1)
                    e.wait_ge(*V["s_min"](l, m))
                    e.activation(sg[m % 2], sg[m % 2], ACT.Exp).then_inc(V["s_sigmoid"].sem, 1)
                if n - 2 in NORM:
                    m = NORM.index(n - 2)
                    if m < 8:
                        e.wait_ge(*V["silu"](l, m))
                    else:
                        e.wait_ge(*V["kept"](l, m - 8))
                    if m >= 2:
                        e.wait_ge(*V["square_sum"](l, m - 2))
                    e.activation(sqr[m % 2], home(n - 2), ACT.Square).then_inc(V["squared"].sem, 1)
                if n - 3 in NORM:
                    m = NORM.index(n - 3)
                    stick = m >= 8
                    e.wait_ge(*V["square_sum"](l, m))
                    if m >= 2:
                        e.wait_ge(*V["normed"](l, m - 2))
                    e.activation(rr[m % 2], bank[2 + m % 2][:], ACT.Ln, bias=eps, scale=1.0 / P if stick else 1.0)\
                     .then_inc(V["ln_sum"].sem, 1)
                    e.wait_ge(*V["ln_sum"](l, m))
                    bias = ln_scale if m < 4 or 8 <= m < 12 else 0.0
                    e.activation(rr[m % 2], rr[m % 2], ACT.Exp, scale=-0.5, bias=bias).then_inc(V["rnorm"].sem, 1)
            mix1_attention_act(e, l, r0, u0)
            mix1_delta_act(e, l, r0, u0)
            for n in range(PAIRS):
                for i in (0, 1):
                    m = N1 + 2 * n + i + 2
                    if N1 + 3 <= m < U_MIX1:
                        split_hi(e, unit(r0, u0 + m))
                    if i == 0:
                        wait_unit(e, r0, u0, N1 + 2 * n)
                        if n:
                            e.wait_ge(*V["p_scaled"](l, n - 1))
                        e.activation(sgm, bank[0][:], ACT.Abs).then_inc(V["p_abs"].sem, 1)
                        e.wait_ge(*V["p_abs"](l, n))
                        e.activation(sgm, sgm, ACT.Exp, scale=-1.0).then_inc(V["p_exp"].sem, 1)
                        e.wait_ge(*V["p_exp"](l, n))
                        e.activation(sgm, sgm, ACT.Ln, bias=one).then_inc(V["p_ln"].sem, 1)
                    else:
                        e.wait_ge(*V["p_min"](l, n))
                        e.activation(sgm, sgm, ACT.Exp).then_inc(V["p_sigmoid"].sem, 1)
                if n == 3:
                    oa_act(e, l, r0, u0)
            for g in range(4):
                e.wait_ge(*V["p_merged"](l, 4 + g))
                wait_unit(e, r0, u0, 42)
                e.activation(xhi[:, 2 * g:2 * g + 2, :], merged[:, 2 * g:2 * g + 2, :], ACT.Copy).then_inc(V["m_hi"].sem, 1)
            split_hi(e, unit(r0, u0 + 46))
            split_hi(e, unit(r0, u0 + 47))

        def oa_act(e, l, r0, u0):
            wait_unit(e, r0, u0, N1 + 7)
            for g in range(GROUPS):
                e.wait_ge(*V["od_gated"](l, g))
                e.activation(yhi[:, 2 * g:2 * g + 2, :], qT[:, 2 * g:2 * g + 2, :], ACT.Copy).then_inc(V["oa_hi"].sem, 1)

        def mix1_dve(e, l, r0, u0, j):
            split_lo(e, unit(r0, u0))
            split_lo(e, unit(r0, u0 + 1))
            e.wait_ge(*V["ba_hi_done"](l))
            e.tensor_tensor(ba_lo[:], ba_raw[:], ba_hi[:].bitcast(F32), ALU.subtract).then_inc(V["ba_lo_done"].sem, 1)
            norm_dve(e, j, lambda c: col("mix_norm", l, c))
            for n in range(N1 + 3):
                if n + 2 <= N1 + 2:
                    split_lo(e, unit(r0, u0 + n + 2))
                if n < 12:
                    kind, g = n // 4, n % 4
                    e.wait_ge(*V["pre_copied"](l, n))
                    e.wait_ge(xt_done, j * 4 + 4)
                    for tap in (3, 2, 1, 0):
                        for b in range(2):
                            o = HOME[kind][:, 2 * g + b, :]
                            w = conv_w[:, bass.ds(l * 96 + (tap * 24 + kind * 8 + 2 * g + b), 1)]
                            src = pre[n % 2][:, b, tap:tap + T]
                            if tap == 3:
                                ins = e.tensor_scalar(o, src, w, None, ALU.mult)
                            else:
                                if b == 0:
                                    e.wait_ge(*V["tap"](l, n * 4 + 2 - tap))
                                ins = e.scalar_tensor_tensor(o, src, w, o, ALU.mult, ALU.add)
                        ins.then_inc(V["tap"].sem, 1)
                if n == 0:
                    small_dve_1(e, l)
                if n == 1:
                    small_dve_2(e, l)
                if n - 1 in SILU:
                    m = SILU.index(n - 1)
                    e.wait_ge(*V["s_ln"](l, m))
                    e.scalar_tensor_tensor(sg[m % 2], home(n - 1), 0.0, sg[m % 2], ALU.min, ALU.subtract)\
                     .then_inc(V["s_min"].sem, 1)
                if n - 3 in NORM:
                    m = NORM.index(n - 3)
                    e.wait_ge(*V["rnorm"](l, m))
                    h = home(n - 3)
                    if m < 8:
                        e.tensor_tensor(h, h, rr[m % 2], ALU.mult).then_inc(V["normed"].sem, 1)
                    else:
                        e.scalar_tensor_tensor(h, h, col("sb_q_norm" if m < 12 else "sb_k_norm", l), rr[m % 2],
                                               ALU.mult, ALU.mult).then_inc(V["normed"].sem, 1)
            mix1_attention_dve(e, l, r0, u0)
            mix1_delta_dve(e, l)
            for n in range(PAIRS):
                for i in (0, 1):
                    m = N1 + 2 * n + i + 2
                    if N1 + 3 <= m < U_MIX1:
                        split_lo(e, unit(r0, u0 + m))
                    if i == 0:
                        e.wait_ge(*V["p_ln"](l, n))
                        e.scalar_tensor_tensor(sgm, bank[0][:], 0.0, sgm, ALU.min, ALU.subtract).then_inc(V["p_min"].sem, 1)
                    else:
                        g = n % 4
                        e.wait_ge(*V["p_sigmoid"](l, n))
                        wait_unit(e, r0, u0, N1 + 2 * n + 1)
                        mg = merged[:, 2 * g:2 * g + 2, :].rearrange("p h t -> p (h t)")
                        if n < 4:
                            e.tensor_tensor(mg, sgm, bank[1][:], ALU.mult).then_inc(V["p_scaled"].sem, 1)
                            e.wait_ge(*V["p_scaled"](l, n))
                            e.sem_inc(V["p_merged"].sem)
                        else:
                            e.wait_ge(*V["p_merged"](l, n - 1))
                            e.tensor_tensor(ytmp, sgm, bank[1][:], ALU.mult).then_inc(V["p_scaled"].sem, 1)
                            e.wait_ge(*V["p_scaled"](l, n))
                            e.tensor_tensor(mg, mg, ytmp, ALU.add).then_inc(V["p_merged"].sem, 1)
                if n == 3:
                    for g in range(GROUPS):
                        e.wait_ge(*V["oa_hi"](l, g))
                        e.tensor_tensor(ylo[:, 2 * g:2 * g + 2, :], qT[:, 2 * g:2 * g + 2, :],
                                        yhi[:, 2 * g:2 * g + 2, :].bitcast(F32), ALU.subtract).then_inc(V["oa_lo"].sem, 1)
            for g in range(4):
                e.wait_ge(*V["m_hi"](l, g))
                e.tensor_tensor(xlo[:, 2 * g:2 * g + 2, :], merged[:, 2 * g:2 * g + 2, :],
                                xhi[:, 2 * g:2 * g + 2, :].bitcast(F32), ALU.subtract).then_inc(V["m_lo"].sem, 1)
            split_lo(e, unit(r0, u0 + 46))
            split_lo(e, unit(r0, u0 + 47))
            add_rows(e, unit(r0, u0 + 47), 1.0)

        def b_of(x):
            return x.rearrange("p (t n) -> p t n", t=TT)[:, :, 0:HEADS]

        def a_of(x):
            return x.rearrange("p (t n) -> p t n", t=TT)[:, :, HEADS:2 * HEADS]

        def th(x):
            return x[:, 0:16].rearrange("p (t h) -> p t h", t=TT)

        def small_act_1(e, l):
            e.wait_ge(*V["ba_product"](l))
            e.activation(ba, bank[2][:, 0:32], ACT.Copy).then_inc(V["ba_kept"].sem, 1)
            e.wait_ge(*V["ba_kept"](l))
            e.activation(th(bt), b_of(ba), ACT.Exp, scale=-1.0).then_inc(V["exp_b"].sem, 1)
            e.wait_ge(*V["a_shift"](l))
            e.activation(bt[:, 16:32], bu[:, 0:16], ACT.Abs).then_inc(V["abs_a"].sem, 1)
            e.wait_ge(*V["abs_a"](l))
            e.activation(bt[:, 16:32], bt[:, 16:32], ACT.Exp, scale=-1.0).then_inc(V["exp_a"].sem, 1)
            e.wait_ge(*V["exp_a"](l))
            e.activation(bt[:, 16:32], bt[:, 16:32], ACT.Ln, bias=one).then_inc(V["ln_a"].sem, 1)
            e.activation(gg[:, 16:24], a_log[:, bass.ds(l * HEADS, HEADS)], ACT.Exp).then_inc(V["exp_alog"].sem, 1)

        def small_dve_1(e, l):
            e.wait_ge(*V["exp_b"](l))
            e.tensor_scalar(bt[:, 0:16], bt[:, 0:16], 1.0, None, ALU.add).then_inc(V["one_b"].sem, 1)
            e.wait_ge(*V["one_b"](l))
            e.reciprocal(beta[:, 0:16], bt[:, 0:16]).then_inc(V["beta_done"].sem, 1)
            for t in range(TT):
                up = e.tensor_tensor(bu[:, t * 8:t * 8 + 8], ba[:, t * 16 + 8:t * 16 + 16],
                                     dt_bias[:, bass.ds(l * HEADS, HEADS)], ALU.add)
            up.then_inc(V["a_shift"].sem, 1)
            e.wait_ge(*V["ln_a"](l))
            e.scalar_tensor_tensor(bu[:, 16:32], bu[:, 0:16], 0.0, bt[:, 16:32], ALU.max, ALU.add)\
             .then_inc(V["softplus_a"].sem, 1)
            e.wait_ge(*V["softplus_a"](l))
            e.wait_ge(*V["exp_alog"](l))
            for t in range(TT):
                up = e.scalar_tensor_tensor(gg[:, t * 8:t * 8 + 8], bu[:, 16 + t * 8:24 + t * 8], -1.0, gg[:, 16:24],
                                            ALU.mult, ALU.mult)
            up.then_inc(V["g_done"].sem, 1)

        def small_act_2(e, l):
            e.wait_ge(*V["cum_product"](l))
            e.activation(cum[:, 0:16], bank[2][:, 0:16], ACT.Copy).then_inc(V["cum_kept"].sem, 1)
            e.wait_ge(*V["cum_kept"](l))
            e.activation(cum[:, 16:32], cum[:, 0:16], ACT.Exp).then_inc(V["exp_cum"].sem, 1)

        def small_dve_2(e, l):
            e.wait_ge(*V["exp_cum"](l))
            e.tensor_tensor(ebg[:, 0:16], cum[:, 16:32], beta[:, 0:16], ALU.mult).then_inc(V["ebg_done"].sem, 1)

        def mix1_attention_pe(e, l):
            for h in range(HEADS + 2):
                if h < HEADS:
                    zb = bank[4 + h % 2]
                    if h == 0:
                        e.wait_ge(*V["normed"](l, 15))
                    if h >= 2:
                        e.wait_ge(*V["z_kept"](l, h - 2))
                    e.matmul(zb[:, 0:256], skT[:, h, 0:P], sqT[:, h, :], start=True, stop=True)
                    e.matmul(zb[:, 256:384], skT[:, h, P:T], sqT[:, h, P:T], start=True, stop=True)\
                     .then_inc(V["z_product"].sem, 1)
                if 0 <= h - 1 < HEADS:
                    g = h - 1
                    sp = att[g % 2][1]
                    e.wait_ge(*V["sp_masked"](l, g))
                    if g:
                        e.wait_ge(*V["z_minus"](l, g - 1))
                    R = bank[6]
                    e.matmul(R[:, 0:256], ge, sp[:, 0:256], start=True, stop=False, skip_group_check=True)
                    e.matmul(R[:, 128:256], ones, sp[:, 256:384], start=False, stop=True, skip_group_check=True)
                    e.matmul(R[:, 256:384], ge, sp[:, 256:384], start=True, stop=True, skip_group_check=True)\
                     .then_inc(V["r_product"].sem, 1)
                if h - 2 >= 0:
                    g = h - 2
                    w = att[g % 2][2]
                    e.wait_ge(*V["w_masked"](l, g))
                    if g == 0:
                        e.wait_ge(*V["kept"](l, 11))
                    if g:
                        e.wait_ge(*V["o_lo"](l, g - 1))
                    e.matmul(bank[7][:, 0:256], sv[:, 0, g * P:(g + 1) * P], w[:, 0:256], start=True, stop=False,
                             skip_group_check=True)
                    e.matmul(bank[7][:, 128:256], sv[:, 1, g * P:(g + 1) * P], w[:, 256:384], start=False, stop=True,
                             skip_group_check=True).then_inc(V["o_product"].sem, 1)

        def mix1_attention_act(e, l, r0, u0):
            for h in range(HEADS + 2):
                if h < HEADS:
                    z, sp, w = att[h % 2]
                    e.wait_ge(*V["z_product"](l, h))
                    if h >= 2:
                        e.wait_ge(*V["w_exp"](l, h - 2))
                        e.wait_ge(*V["r_product"](l, h - 2))
                    e.activation(z, bank[4 + h % 2][:, 0:384], ACT.Copy).then_inc(V["z_kept"].sem, 1)
                    e.wait_ge(*V["z_kept"](l, h))
                    e.activation(sp, z, ACT.Abs).then_inc(V["z_abs"].sem, 1)
                    e.wait_ge(*V["z_abs"](l, h))
                    e.activation(sp, sp, ACT.Exp, scale=-1.0).then_inc(V["z_exp"].sem, 1)
                    e.wait_ge(*V["z_exp"](l, h))
                    e.activation(sp, sp, ACT.Ln, bias=one).then_inc(V["z_ln"].sem, 1)
                if 0 <= h - 1 < HEADS:
                    g = h - 1
                    z, sp, w = att[g % 2]
                    e.wait_ge(*V["z_minus"](l, g))
                    if g >= 2:
                        e.wait_ge(*V["o_product"](l, g - 2))
                    e.activation(w, z, ACT.Exp).then_inc(V["w_exp"].sem, 1)
                if h - 2 >= 0:
                    g = h - 2
                    e.wait_ge(*V["o_product"](l, g))
                    e.activation(yhi[:, g, :], bank[7][:, 0:256], ACT.Copy).then_inc(V["o_hi"].sem, 1)

        def mix1_attention_dve(e, l, r0, u0):
            for h in range(HEADS + 2):
                if h < HEADS:
                    z, sp, w = att[h % 2]
                    e.wait_ge(*V["z_ln"](l, h))
                    e.scalar_tensor_tensor(sp, z, 0.0, sp, ALU.max, ALU.add).then_inc(V["softplus"].sem, 1)
                if 0 <= h - 1 < HEADS:
                    g = h - 1
                    z, sp, w = att[g % 2]
                    e.wait_ge(*V["r_product"](l, g))
                    e.tensor_tensor(z, z, bank[6][:, 0:384], ALU.subtract).then_inc(V["z_minus"].sem, 1)
                if h - 2 >= 0:
                    g = h - 2
                    e.wait_ge(*V["o_hi"](l, g))
                    e.tensor_tensor(ylo[:, g, :], bank[7][:, 0:256], yhi[:, g, :].bitcast(F32), ALU.subtract)\
                     .then_inc(V["o_lo"].sem, 1)

        def finish_waits(e):
            e.sem_inc(pool_waited)

        def keep_earlier_keys(e, a):
            for c in (0, 256):
                up = e.affine_select(out=a[:, c:c + P], in_=a[:, c:c + P], compare_op=ALU.is_gt, fill=0.0, base=0,
                                     pattern=[[1, P]], channel_multiplier=-1)
            return up

        def mix1_attention_pool(e, l):
            for h in range(HEADS + 1):
                if h < HEADS:
                    e.wait_ge(*V["softplus"](l, h))
                    finish_waits(e)
                    keep_earlier_keys(e, att[h % 2][1]).then_inc(V["sp_masked"].sem, 1)
                if h - 1 >= 0:
                    e.wait_ge(*V["w_exp"](l, h - 1))
                    finish_waits(e)
                    keep_earlier_keys(e, att[(h - 1) % 2][2]).then_inc(V["w_masked"].sem, 1)

        def tile_col(a, g, i):
            c = (i % 2) * 8 + 2 * g + i // 2
            return a[:, c:c + 1]

        def mix1_delta_pe(e, l):
            e.wait_ge(*V["o_lo"](l, HEADS - 1))
            e.wait_ge(*V["silu"](l, 15))
            for g in range(GROUPS):
                e.wait_ge(*V["g_spread"](l, g))
                e.matmul(bank[g][:], ones, Mb[g].rearrange("p i n -> p (i n)"), start=True, stop=True)\
                 .then_inc(V["g_rows"].sem, 1)
                for i in range(4):
                    h, t = 2 * g + i // 2, i % 2 * P
                    mm = e.matmul(b4(4 + g)[:, i, :], kT[:, h, t:t + P], kT[:, h, t:t + P], start=True, stop=True)
                mm.then_inc(V["kk"].sem, 1)
            for g in range(GROUPS):
                e.wait_ge(*V["x_abs"](l, g))
                e.wait_ge(*V["glast_kept"](l, g))
                for i in range(4):
                    h, t = 2 * g + i // 2, i % 2 * P
                    mm = e.matmul(b4(g)[:, i, :], kT[:, h, t:t + P], qT[:, h, t:t + P], start=True, stop=True)
                mm.then_inc(V["qk"].sem, 1)
            for s in range(LEVELS):
                for g in range(GROUPS):
                    e.wait_ge(*V["m_ready"](l, s * 4 + g))
                    if s == 0:
                        e.wait_ge(*V["attn_done"](l, g))
                        for i in range(4):
                            mm = e.matmul(b4(g)[:, i, :], Mb[g][:, i, :], ident, start=True, stop=True)
                        mm.then_inc(V["tu_product"].sem, 1)
                    else:
                        for i in range(4):
                            mm = e.matmul(b4(g)[:, i, :], Mb[g][:, i, :], Ub[g][:, i, :], start=True, stop=True)
                        mm.then_inc(V["m_product"].sem, 1)
                if s:
                    for g in range(GROUPS):
                        e.wait_ge(*V["w_kept"](l, s * 4 - 4 + g))
                        for i in range(4):
                            mm = e.matmul(b4(g)[:, i, :], Tb[g][:, i, :], Mb[g][:, i, :], start=True, stop=True)
                        if s < LEVELS - 1:
                            for i in range(4):
                                mm = e.matmul(b4(4 + g)[:, i, :], Mb[g][:, i, :], Tb[g][:, i, :], start=True, stop=True)
                        mm.then_inc(V["tu_product"].sem, 1)
            for g in range(GROUPS):
                e.wait_ge(*V["tu_done"](l, 24 + g))
                for i in range(4):
                    h, t = 2 * g + i // 2, i % 2 * P
                    e.transpose(b4(g)[:, i, :], kT[:, h, t:t + P], ident)
                    mm = e.transpose(b4(4 + g)[:, i, :], vT[:, h, t:t + P], ident)
                mm.then_inc(V["kv_turned"].sem, 1)
            for g in range(GROUPS):
                e.wait_ge(*V["k_scaled"](l, g))
                e.wait_ge(*V["v_scaled"](l, g))
                for i in range(4):
                    mm = e.matmul(b4(g)[:, i, :], Ub[g][:, i, :], Tb[g][:, i, :], start=True, stop=True)
                for hh in range(2):
                    mm = e.matmul(b4(4 + g)[:, hh, :], Mb[g][:, 2 * hh + 1, :], Ub[g][:, 2 * hh + 1, :], start=True, stop=True)
                mm.then_inc(V["uw_product"].sem, 1)
            for g in range(GROUPS):
                e.wait_ge(*V["u_kept"](l, g))
                e.wait_ge(*V["w_copied"](l, g))
                for hh in range(2):
                    mm = e.matmul(b4(4 + g)[:, 2 + hh, :], vT[:, 2 * g, hh * P:(hh + 1) * P], Lb[g][:, 2 * hh, :],
                                  start=True, stop=True)
                mm.then_inc(V["s_product"].sem, 1)
            for g in range(GROUPS):
                e.wait_ge(*V["s_kept"](l, g))
                for hh in range(2):
                    mm = e.matmul(b4(4 + g)[:, hh, :], kT[:, 2 * g, hh * P:(hh + 1) * P],
                                  kT[:, 2 * g + 1, hh * P:(hh + 1) * P], start=True, stop=True)
                mm.then_inc(V["ws_product"].sem, 1)
            for g in range(GROUPS):
                e.wait_ge(*V["v_new"](l, g))
                e.wait_ge(*V["q_decayed"](l, g))
                for hh in range(2):
                    o = b2(g)[:, hh, :]
                    e.matmul(o[:, 0:P], Lb[g][:, 2 * hh, :], Ab[g][:, 2 * hh, :], start=True, stop=True)
                    e.matmul(o[:, P:T], kT[:, 2 * g + 1, hh * P:(hh + 1) * P], qT[:, 2 * g + hh, P:T], start=True,
                             stop=False)
                    mm = e.matmul(o[:, P:T], vT[:, 2 * g + 1, hh * P:(hh + 1) * P], Ab[g][:, 2 * hh + 1, :],
                                  start=False, stop=True)
                mm.then_inc(V["od_product"].sem, 1)
            for g in range(GROUPS):
                e.wait_ge(*V["od_squared"](l, g))
                e.matmul(bank[4 + g][:], ones, Mb[g].rearrange("p i n -> p (i n)"), start=True, stop=True)\
                 .then_inc(V["od_sum"].sem, 1)

        def flat(a):
            return a.rearrange("p i n -> p (i n)")

        def mix1_delta_act(e, l, r0, u0):
            for g in range(GROUPS):
                e.wait_ge(*V["g_rows"](l, g))
                e.wait_ge(*V["o_lo"](l, HEADS - 1))
                for hh in range(2):
                    up = e.activation(egb[g][:, hh, :], b4(g)[:, 2 * hh + 1, :], ACT.Exp)
                up.then_inc(V["egb_done"].sem, 1)
                for i in range(4):
                    up = e.activation(Ab[g][:, i, :], b4(g)[:, i, :], ACT.Abs, scale=-1.0, bias=tile_col(cum, g, i))
                up.then_inc(V["x_abs"].sem, 1)
                e.wait_ge(*V["x_abs"](l, g))
                e.activation(flat(Mb[g]), flat(Ab[g]), ACT.Exp, scale=-1.0).then_inc(V["decay"].sem, 1)
                e.wait_ge(*V["glast_kept"](l, g))
                e.activation(ekd[:, 2 * g:2 * g + 2], glast[:, 2 * g:2 * g + 2], ACT.Exp).then_inc(V["ekd_done"].sem, 1)
            for s in range(1, LEVELS):
                for g in range(GROUPS):
                    e.wait_ge(*V["m_product"](l, s * 4 - 4 + g))
                    e.activation(flat(Mb[g]), bank[g][:], ACT.Copy).then_inc(V["w_kept"].sem, 1)
            for g in range(GROUPS):
                e.wait_ge(*V["kv_turned"](l, g))
                e.wait_ge(*V["ebg_done"](l))
                for i in range(4):
                    e.activation(Mb[g][:, i, :], b4(g)[:, i, :], ACT.Copy, scale=tile_col(ebg, g, i))
                e.wait_ge(*V["ekd_done"](l, g))
                for hh in range(2):
                    up = e.activation(vT[:, 2 * g, hh * P:(hh + 1) * P], b4(g)[:, 2 * hh, :], ACT.Copy,
                                      scale=ekd[:, 2 * g + hh:2 * g + hh + 1])
                up.then_inc(V["k_scaled"].sem, 1)
            for g in range(GROUPS):
                e.wait_ge(*V["uw_product"](l, g))
                e.activation(kT[:, 2 * g, :], bank[4 + g][:, 0:256], ACT.Copy).then_inc(V["w_copied"].sem, 1)
            for g in range(GROUPS):
                e.wait_ge(*V["s_product"](l, g))
                e.activation(kT[:, 2 * g + 1, :], bank[4 + g][:, 256:512], ACT.Copy).then_inc(V["s_kept"].sem, 1)
            for g in range(GROUPS):
                e.wait_ge(*V["od_product"](l, g))
                e.activation(flat(Mb[g]), bank[g][:], ACT.Square).then_inc(V["od_squared"].sem, 1)
            for g in range(GROUPS):
                e.wait_ge(*V["od_sum"](l, g))
                e.activation(flat(Tb[g]), bank[4 + g][:], ACT.Ln, bias=eps, scale=1.0 / P).then_inc(V["od_ln"].sem, 1)
                e.wait_ge(*V["od_ln"](l, g))
                e.activation(flat(Tb[g]), flat(Tb[g]), ACT.Exp, scale=-0.5).then_inc(V["od_r"].sem, 1)

        def mix1_delta_dve(e, l):
            for g in range(GROUPS):
                e.wait_ge(*V["g_rows"](l, g))
                e.wait_ge(*V["x_abs"](l, g))
                for hh in range(2):
                    up = e.tensor_tensor(glast[:, 2 * g + hh:2 * g + hh + 1], b4(g)[:, 2 * hh, P - 1:P],
                                         tile_col(cum, g, 2 * hh), ALU.subtract)
                up.then_inc(V["glast_kept"].sem, 1)
            for g in range(GROUPS):
                e.wait_ge(*V["kk"](l, g))
                e.wait_ge(*V["decay"](l, g))
                e.wait_ge(*V["beta_done"](l))
                for i in range(4):
                    up = e.scalar_tensor_tensor(Lb[g][:, i, :], b4(4 + g)[:, i, :], tile_col(beta, g, i), Mb[g][:, i, :],
                                                ALU.mult, ALU.mult)
                up.then_inc(V["l_done"].sem, 1)
                e.wait_ge(*V["a_mask"](l, g))
                e.wait_ge(*V["qk"](l, g))
                e.tensor_tensor(flat(Ab[g]), bank[g][:], flat(Ab[g]), ALU.mult).then_inc(V["attn_done"].sem, 1)
            for s in range(LEVELS):
                for g in range(GROUPS):
                    e.wait_ge(*V["tu_product"](l, s * 4 + g))
                    if s == 0:
                        for i in range(4):
                            e.tensor_tensor(Tb[g][:, i, :], ident, Mb[g][:, i, :], ALU.subtract)
                            up = e.scalar_tensor_tensor(Ub[g][:, i, :], b4(g)[:, i, :], -1.0, ident, ALU.mult, ALU.add)
                    else:
                        if s < LEVELS - 1:
                            e.tensor_tensor(flat(Tb[g]), flat(Tb[g]), bank[4 + g][:], ALU.subtract)
                        up = e.tensor_tensor(flat(Ub[g]), flat(Ub[g]), bank[g][:], ALU.subtract)
                    up.then_inc(V["tu_done"].sem, 1)
            for g in range(GROUPS):
                e.wait_ge(*V["kv_turned"](l, g))
                for i in range(4):
                    up = e.tensor_scalar(Tb[g][:, i, :], b4(4 + g)[:, i, :], tile_col(beta, g, i), None, ALU.mult)
                up.then_inc(V["v_scaled"].sem, 1)
            for g in range(GROUPS):
                e.wait_ge(*V["uw_product"](l, g))
                e.tensor_copy(flat(Lb[g]), bank[g][:]).then_inc(V["u_kept"].sem, 1)
            for g in range(GROUPS):
                e.wait_ge(*V["ws_product"](l, g))
                e.wait_ge(*V["u_kept"](l, g))
                e.tensor_tensor(vT[:, 2 * g + 1, :].rearrange("p (h n) -> p h n", h=2), Lb[g][:, 1:4:2, :],
                                b4(4 + g)[:, 0:2, :], ALU.subtract).then_inc(V["v_new"].sem, 1)
            for g in range(GROUPS):
                e.wait_ge(*V["od_r"](l, g))
                o = qT[:, 2 * g:2 * g + 2, :].rearrange("p h t -> p (h t)")
                e.scalar_tensor_tensor(o, bank[g][:], col("dn_out_norm", l), flat(Tb[g]), ALU.mult, ALU.mult)\
                 .then_inc(V["od_norm"].sem, 1)

        def mix1_pool(e, l):
            for m, n in enumerate(SILU):
                e.wait_ge(*V["s_sigmoid"](l, m))
                e.tensor_tensor(home(n), home(n), sg[m % 2], ALU.mult).then_inc(V["silu"].sem, 1)
            mix1_attention_pool(e, l)
            for g in range(GROUPS):
                e.wait_ge(*V["g_done"](l))
                e.wait_ge(*V["o_lo"](l, HEADS - 1))
                finish_waits(e)
                for i in range(4):
                    up = e.tensor_scalar(Mb[g][:, i, :], le, tile_col(gg, g, i), None, ALU.mult)
                up.then_inc(V["g_spread"].sem, 1)
            for g in range(GROUPS):
                e.wait_ge(*V["decay"](l, g))
                for i in range(4):
                    up = e.tensor_tensor(Ab[g][:, i, :], Mb[g][:, i, :], le, ALU.mult)
                up.then_inc(V["a_mask"].sem, 1)
            for s in range(LEVELS):
                for g in range(GROUPS):
                    if s == 0:
                        e.wait_ge(*V["l_done"](l, g))
                        e.wait_ge(*V["a_mask"](l, g))
                    else:
                        e.wait_ge(*V["tu_done"](l, s * 4 - 4 + g))
                    for i in range(4):
                        up = e.tensor_tensor(Mb[g][:, i, :], Lb[g][:, i, :], const(f"level{s}"), ALU.mult)
                    up.then_inc(V["m_ready"].sem, 1)
            for g in range(GROUPS):
                e.wait_ge(*V["egb_done"](l, g))
                e.wait_ge(*V["qk"](l, g))
                q2 = qT[:, 2 * g:2 * g + 2, P:T]
                e.tensor_tensor(q2, q2, egb[g], ALU.mult).then_inc(V["q_decayed"].sem, 1)
            for g in range(GROUPS):
                e.wait_ge(*V["od_norm"](l, g))
                o = qT[:, 2 * g:2 * g + 2, :]
                e.tensor_tensor(o, o, zT[:, 2 * g:2 * g + 2, :], ALU.mult).then_inc(V["od_gated"].sem, 1)

        IN2 = ("aq", "ak", "av", "bq", "bkv", "cq", "ck", "cv", "dval", "dgate")
        IN2_COL = (0, 256, 512, 768, 1024, 1184, 1440, 1696, 1956, 2212)
        CF_COL = 1952
        G2, B2, O2 = 10, 26, 30
        HD = 64
        H2 = 4

        def blk(a, n=512):
            return arena[:, a:a + n]

        gates = arena[:, 0:8192].rearrange("p (u n) -> p u n", n=512)
        bias_a = blk(5120, 1024).rearrange("p (h t) -> p h t", h=H2)
        w_uq = blk(6144, 768).rearrange("p (c n) -> p c n", c=2)
        w_ukv = blk(6912, 512)
        aq, ak, bqlat, bkv, cq, ck = [blk(a).rearrange("p (c t) -> p c t", c=2)
                                      for a in (8192, 8704, 9728, 10240, 10752, 11264)]
        av, cv, bv = [blk(a).rearrange("p (t n) -> p t n", t=TT) for a in (9216, 11776, 15424)]
        CONV_K = 31
        dpad = blk(12288, 2 * (T + CONV_K - 1)).rearrange("p (c t) -> p c t", c=2)
        dgate = blk(12864)
        bqh = blk(13376, 1024).rearrange("p (h t) -> p h t", h=H2)
        bkh = blk(14400, 1024).rearrange("p (h t) -> p h t", h=H2)
        Pb = [blk(15936 + i * 384, 384) for i in range(2)]
        PTb = [blk(16704 + i * 384, 384) for i in range(2)]
        rtmp = blk(17472)
        CG = [blk(17984 + i * 384, 384) for i in range(2)]
        table2 = blk(18944, CONSTANTS2.shape[1])
        cy, csq, cr = blk(13376), blk(13888), blk(14400)
        gtmp = [blk(14912 + i * 512) for i in range(2)]
        ytmp2 = [blk(15936 + i * 512) for i in range(2)]
        merged2 = blk(8192, 2048).rearrange("p (c t) -> p c t", t=T)
        lat_sq = [blk(13376), blk(13888)]
        lat_r = blk(14400)
        rtmp2 = blk(7424)
        cos_t = rotary[:, 0:T]
        sin_t = rotary[:, T:2 * T]

        def const2(name):
            a, b = CONST2_AT[name]
            return table2[:, a:b]

        ones2, minus, mask_chunk, mask_causal, turn, freq = [const2(n) for n in
                                                             ("ones2", "minus", "chunk", "causal", "turn", "freq")]
        cf_raw, cf_hi, cf_lo = [w[:, :, 0:H2] for w in ba_w]
        cfy, cfe, lf = small[:, 0:8], small[:, 8:16], small[:, 16:24]
        stats = small[:, 32:32 + 12 * 8]

        small_in = sem("small_in")
        spare = iter(V.values())
        W = {n: next(spare).reused(p) for n, p in dict(
            cf_hi=1, cf_lo=1, cf_product=1, cf_kept=1, cf_abs=1, cf_exp=1, cf_ln=1, lf=1,
            kept=10, d_abs=1, d_exp=1, d_ln=1, d_min=1, d_sig=1, u_done=1, lat_sq=2, lat_sum=1, lat_ln=1, lat_r=1,
            lat_n=1, up_product=2, up_kept=2, v_product=1, v_kept=1, turned=3, rope_sin=3, rope_done=3, pads=1, lf_shift=1, rowmax=12, bias_masked=1, k_tmp=1,
            cg=4, scores=12, maxed=12, expd=12, inv=12, scaled=12, p_turned=12, pt_kept=12, o_product=12, o_hi=6, o_lo=6,
            tap=31, mean=1, centred=1, c_sq=1, c_var=1, c_ln=1, c_r=1, c_norm=1, c_bias=1, c_abs=1, c_exp=1, c_l=1,
            c_min=1, c_sig=1, c_out=1, c_hi=1, c_lo=1,
            g_bias=16, g_abs=16, g_exp=16, g_ln=16, g_min=16, g_sig=16, y_scaled=16, y_added=16, m_hi=4, m_lo=4,
            relu=16, square=16, h_hi=16, h_lo=16).items()}

        def mix2_sync(e, l, r0, u0, j):
            w = d["w_in_2"]

            def columns(w, c):
                return w[l, :, c:c + 256].rearrange("(c p) n -> p c n", p=P)

            for n in range(10):
                if n == 3:
                    e.wait_ge(x_new[1], 1 + j)
                    e.dma_start(ba_raw[:, :, 0:H2], w[l, :, CF_COL:CF_COL + H2].rearrange("(c p) n -> p c n", p=P))\
                     .then_inc(small_in, 16)
                    e.dma_start(w_uq, d["w_uq_2"][l].rearrange("(c p) n -> p c n", p=P)).then_inc(small_in, 16)
                    e.dma_start(w_ukv, d["w_ukv_2"][l]).then_inc(small_in, 16)
                    e.dma_start(bias_a, bias_rows[l].rearrange("h s m -> h (s m)")[:, P:P + P * 383]
                                .rearrange("h (s m) -> s h m", m=383)[:, :, 0:T]).then_inc(small_in, 16)
                load_unit(e, unit(r0, u0 + n), columns(w, IN2_COL[n]), as_in)
            for n in range(4):
                for q in range(4):
                    load_unit(e, unit(r0, u0 + G2 + 4 * n + q), columns(d["w_gate_2"], n * D + q * 256), as_in)
            for n in range(4):
                load_unit(e, unit(r0, u0 + B2 + n), d["w_branch_2"][l, n].rearrange("(c p) n -> p c n", p=P), as_out)
            for g in range(4):
                load_unit(e, unit(r0, u0 + O2 + g),
                          d["w_o_2"][l, g * 256:(g + 1) * 256, :].rearrange("(c p) n -> p c n", p=P), as_out)

        def scores_a(e, h, o):
            p = slice(HD * (h % 2), HD * (h % 2) + HD)
            b = h // 2
            e.matmul(o[:, 0:128], aq[p, b, 0:P], ak[p, b, 0:P], start=True, stop=False, skip_group_check=True)
            e.matmul(o[:, 0:128], bias_a[:, h, 0:P], ident, start=False, stop=True, skip_group_check=True)
            e.matmul(o[:, 128:384], aq[p, b, P:T], ak[p, b, :], start=True, stop=False, skip_group_check=True)
            e.matmul(o[:, 128:256], bias_a[:, h, P:T], ident, start=False, stop=True, skip_group_check=True)
            return e.matmul(o[:, 256:384], bias_a[:, h, 0:P], ident, start=False, stop=True, skip_group_check=True)

        def scores_b(e, h, o):
            e.matmul(o[:, 0:128], bqh[0:96, h, 0:P], bkh[0:96, h, 0:P], start=True, stop=False, skip_group_check=True)
            e.matmul(o[:, 0:128], mask_chunk, ident, start=False, stop=True, skip_group_check=True)
            e.matmul(o[:, 128:384], bqh[0:96, h, P:T], bkh[0:96, h, :], start=True, stop=False, skip_group_check=True)
            return e.matmul(o[:, 256:384], mask_chunk, ident, start=False, stop=True, skip_group_check=True)

        def scores_c(e, h, o):
            p = slice(HD * (h % 2), HD * (h % 2) + HD)
            b = h // 2
            G = CG[h % 2]
            k = dict(skip_group_check=True)
            e.matmul(o[:, 0:128], cq[p, b, 0:P], ck[p, b, 0:P], start=True, stop=False, **k)
            e.matmul(o[:, 0:128], G[:, 0:128], ones2[:, 0:P], start=False, stop=False, **k)
            e.matmul(o[:, 0:128], minus, G[:, 0:128], start=False, stop=False, **k)
            e.matmul(o[:, 0:128], mask_causal, ident, start=False, stop=True, **k)
            e.matmul(o[:, 128:384], cq[p, b, P:T], ck[p, b, :], start=True, stop=False, **k)
            e.matmul(o[:, 128:384], G[:, 128:256], ones2, start=False, stop=False, **k)
            e.matmul(o[:, 128:384], G[:, 256:384], ones2, start=False, stop=False, **k)
            e.matmul(o[:, 128:384], minus, G[:, 0:256], start=False, stop=False, **k)
            e.matmul(o[:, 256:384], minus, G[:, 256:384], start=False, stop=False, **k)
            return e.matmul(o[:, 256:384], mask_causal, ident, start=False, stop=True, **k)

        ATT = 12

        def values(hd):
            b, h = hd // 4, hd % 4
            return (av, bv, cv)[b], h

        def mix2_pe(e, l, r0, u0, j):
            norm_pe(e, j)
            norm_ready(e, j)
            e.wait_ge(*W["cf_hi"](l))
            e.wait_ge(*W["cf_lo"](l))
            for t in range(TT):
                for c in range(KC):
                    mm = product3(e, bank[2][:, t * H2:(t + 1) * H2], xhi[:, c, t * P:(t + 1) * P],
                                 xlo[:, c, t * P:(t + 1) * P], cf_hi[:, c, :], cf_lo[:, c, :], c == 0, c == KC - 1)
            mm.then_inc(W["cf_product"].sem, 1)
            for n in range(10):
                if n >= 2:
                    e.wait_ge(*W["kept"](l, n - 2))
                s, _ = unit(r0, u0 + n)
                if IN2[n] in ("av", "cv"):
                    row_unit(e, unit(r0, u0 + n), bank[n % 2], xhi, xlo)
                elif n == 4:
                    split_ready(e, unit(r0, u0 + n))
                    for b in range(2):
                        for c in range(KC):
                            mm = product3(e, bank[n % 2][:, b * T:(b + 1) * T], as_in(whi[s])[:, c, b * 64:b * 64 + P],
                                          as_in(wlo[s])[:, c, b * 64:b * 64 + P], xhi[:, c, :], xlo[:, c, :],
                                          c == 0, c == KC - 1)
                    mm.then_inc(multiplied[s], 1)
                else:
                    feature_product(e, unit(r0, u0 + n), bank[n % 2], xhi, xlo)
                if n == 6:
                    e.wait_ge(*W["lat_sq"](l, 1))
                    e.wait_ge(*W["cf_kept"](l))
                    e.matmul(bank[2][:, 0:T], ones, lat_sq[0][:, 0:T], start=True, stop=False)
                    e.matmul(bank[2][:, 0:T], ones, lat_sq[0][:, T:2 * T], start=False, stop=True)
                    e.matmul(bank[2][:, T:2 * T], ones, lat_sq[1][:, 0:T], start=True, stop=True).then_inc(W["lat_sum"].sem, 1)
                if n == 8:
                    e.wait_ge(*W["lat_n"](l))
                    e.wait_ge(small_in, l * 64 + 64)
                    for h in range(H2):
                        o = bank[3 + h // 2][0:96, h % 2 * T:(h % 2 + 1) * T]
                        for c in range(2):
                            mm = e.matmul(o, w_uq[:, c, h * 96:(h + 1) * 96], bqlat[:, c, :], start=c == 0, stop=c == 1)
                    mm.then_inc(W["up_product"].sem, 1)
                    for h in range(H2):
                        mm = e.matmul(bank[5 + h // 2][0:HD, h % 2 * T:(h % 2 + 1) * T], w_ukv[:, h * P:h * P + HD],
                                      bkv[:, 0, :], start=True, stop=True)
                    mm.then_inc(W["up_product"].sem, 1)
                    for t in range(TT):
                        mm = e.matmul(bank[7][:, t * T:(t + 1) * T], bkv[:, 0, t * P:(t + 1) * P],
                                      w_ukv.rearrange("p (h n) -> p h n", h=H2)[:, :, HD:P], start=True, stop=True)
                    mm.then_inc(W["v_product"].sem, 1)
            e.wait_ge(*W["up_kept"](l, 1))
            for i in range(2):
                e.matmul(bank[3 + i][0:96, :], turn[0:96, :], bqh[0:96, 2 * i:2 * i + 2, :], start=True, stop=True)\
                 .then_inc(W["turned"].sem, 1)
            e.matmul(bank[5][0:96, 0:T], turn[0:96, :], bkv[0:96, 1, :], start=True, stop=True).then_inc(W["turned"].sem, 1)
            for hd in range(ATT + 2):
                if hd < ATT:
                    b, h = hd // 4, hd % 4
                    o = bank[6 + hd % 2]
                    if hd == 0:
                        e.wait_ge(*W["v_kept"](l))
                        e.wait_ge(*W["kept"](l, 1))
                        e.wait_ge(*W["bias_masked"](l))
                    if hd == 4:
                        e.wait_ge(*W["rope_done"](l, 2))
                    if b == 2:
                        e.wait_ge(*W["cg"](l, h))
                        e.wait_ge(*W["kept"](l, 9))
                    if hd >= 2:
                        e.wait_ge(*W["expd"](l, hd - 2))
                    (scores_a, scores_b, scores_c)[b](e, h, o).then_inc(W["scores"].sem, 1)
                if 0 <= hd - 1 < ATT:
                    g = hd - 1
                    e.wait_ge(*W["scaled"](l, g))
                    if g == 0:
                        e.wait_ge(*W["lat_r"](l))
                    else:
                        e.wait_ge(*W["pt_kept"](l, g - 1))
                    for a in range(3):
                        mm = e.transpose(bank[2][:, a * P:(a + 1) * P], Pb[g % 2][:, a * P:(a + 1) * P], ident)
                    mm.then_inc(W["p_turned"].sem, 1)
                if hd - 2 >= 0:
                    g = hd - 2
                    v, h = values(g)
                    e.wait_ge(*W["pt_kept"](l, g))
                    if g == 0:
                        e.wait_ge(*W["kept"](l, 9))
                    if g % 2 == 0 and g >= 2:
                        e.wait_ge(*W["o_lo"](l, g // 2 - 1))
                    o = bank[1][HD * (g % 2):HD * (g % 2) + HD, 0:T]
                    e.matmul(o, v[:, 0, h * HD:(h + 1) * HD], PTb[g % 2][:, 0:T], start=True, stop=False,
                             skip_group_check=True)
                    e.matmul(o[:, P:T], v[:, 1, h * HD:(h + 1) * HD], PTb[g % 2][:, T:384], start=False, stop=True,
                             skip_group_check=True).then_inc(W["o_product"].sem, 1)
            for k in range(16):
                if k >= 2:
                    e.wait_ge(*W["g_bias"](l, k - 2))
                else:
                    e.wait_ge(*W["expd"](l, ATT - 1))
                feature_product(e, unit(r0, u0 + G2 + k), bank[6 + k % 2], xhi, xlo)
                if k == 8:
                    e.wait_ge(*W["tap"](l, 30))
                    e.wait_ge(*W["pt_kept"](l, ATT - 1))
                    e.matmul(bank[2][:, 0:T], ones, cy[:, 0:T], start=True, stop=False)
                    e.matmul(bank[2][:, 0:T], ones, cy[:, T:2 * T], start=False, stop=True).then_inc(W["mean"].sem, 1)
                if k == 9:
                    e.wait_ge(*W["c_sq"](l))
                    e.matmul(bank[2][:, 0:T], ones, csq[:, 0:T], start=True, stop=False)
                    e.matmul(bank[2][:, 0:T], ones, csq[:, T:2 * T], start=False, stop=True).then_inc(W["c_var"].sem, 1)
            for n in range(4):
                s, _ = unit(r0, u0 + B2 + n)
                split_ready(e, unit(r0, u0 + B2 + n))
                if n == 0:
                    e.wait_ge(*W["o_lo"](l, 5))
                    e.wait_ge(*W["g_bias"](l, 15))
                    e.wait_ge(*W["rope_done"](l, 2))
                    e.wait_ge(*W["c_ln"](l))
                if n == 3:
                    e.wait_ge(*W["c_lo"](l))
                for q in range(4):
                    k = 4 * n + q
                    o = bank[k % 8]
                    if k >= 8:
                        e.wait_ge(*W["y_scaled"](l, k - 8))
                    for b in range(2):
                        for c in range(2):
                            m = (2 * q + b) * P
                            mm = product3(e, o[:, b * T:(b + 1) * T], as_out(whi[s])[:, c, m:m + P],
                                          as_out(wlo[s])[:, c, m:m + P], yhi[:, 2 * n + c, :], ylo[:, 2 * n + c, :],
                                          c == 0, c == 1)
                    if q < 3:
                        mm.then_inc(y_product.sem, 1)
                    else:
                        mm.then_inc(multiplied[s], 1)
            e.wait_ge(*W["y_scaled"](l, 11))
            clear_rows(e)
            for g in range(4):
                e.wait_ge(*W["m_lo"](l, g))
                row_product(e, unit(r0, u0 + O2 + g), xhi[:, 2 * g:2 * g + 2, :], xlo[:, 2 * g:2 * g + 2, :], g == 3)

        y_product = ev("b_y_product", 12)

        def y_ready(e, l, r0, u0, k):
            n, q = k // 4, k % 4
            if q < 3:
                e.wait_ge(*y_product(l, n * 3 + q))
            else:
                wait_unit(e, r0, u0, B2 + n)

        KEEP2 = {"aq": aq, "ak": ak, "av": av, "bq": bqlat, "bkv": bkv, "cq": cq, "ck": ck, "cv": cv}

        def mix2_act(e, l, r0, u0, j):
            split_hi(e, unit(r0, u0))
            split_hi(e, unit(r0, u0 + 1))
            norm_act(e, j, lambda c: col("g_mix_2", l, c))
            e.wait_ge(small_in, l * 64 + 64)
            e.activation(cf_hi, cf_raw, ACT.Copy).then_inc(W["cf_hi"].sem, 1)
            for n in range(10):
                split_hi(e, unit(r0, u0 + n + 2))
                wait_unit(e, r0, u0, n)
                src = bank[n % 2][:]
                if n < 8:
                    dst = KEEP2[IN2[n]].rearrange("p c t -> p (c t)")
                    e.activation(dst, src, ACT.Copy, scale=0.125 if IN2[n] in ("aq", "cq") else 1.0).then_inc(W["kept"].sem, 1)
                elif n == 8:
                    e.wait_ge(*W["kept"](l, 7))
                    e.wait_ge(*W["pads"](l))
                    e.activation(dpad[:, :, CONV_K - 1:], b2(n % 2), ACT.Copy).then_inc(W["kept"].sem, 1)
                else:
                    e.activation(dgate, src, ACT.Copy).then_inc(W["kept"].sem, 1)
                if n == 0:
                    e.wait_ge(*W["cf_product"](l))
                    e.activation(cfy, bank[2][:, 0:8], ACT.Copy).then_inc(W["cf_kept"].sem, 1)
                if n == 1:
                    e.wait_ge(*W["lf_shift"](l))
                    e.activation(cfe, cfy, ACT.Abs).then_inc(W["cf_abs"].sem, 1)
                    e.wait_ge(*W["cf_abs"](l))
                    e.activation(cfe, cfe, ACT.Exp, scale=-1.0).then_inc(W["cf_exp"].sem, 1)
                    e.wait_ge(*W["cf_exp"](l))
                    e.activation(cfe, cfe, ACT.Ln, bias=one).then_inc(W["cf_ln"].sem, 1)
                if n == 4:
                    e.wait_ge(*W["kept"](l, 4))
                    e.activation(lat_sq[0], bqlat.rearrange("p c t -> p (c t)"), ACT.Square).then_inc(W["lat_sq"].sem, 1)
                    e.activation(lat_sq[1][:, 0:T], bkv[:, 0, :], ACT.Square).then_inc(W["lat_sq"].sem, 1)
                if n == 7:
                    e.wait_ge(*W["lat_sum"](l))
                    e.activation(lat_r[:, 0:T], bank[2][:, 0:T], ACT.Ln, bias=eps, scale=1.0 / 256)
                    e.activation(lat_r[:, T:2 * T], bank[2][:, T:2 * T], ACT.Ln, bias=eps, scale=1.0 / P)\
                     .then_inc(W["lat_ln"].sem, 1)
                    e.wait_ge(*W["lat_ln"](l))
                    e.activation(lat_r, lat_r, ACT.Exp, scale=-0.5).then_inc(W["lat_r"].sem, 1)
            e.wait_ge(*W["up_product"](l, 0))
            for i in range(2):
                up = e.activation(bqh[0:96, 2 * i:2 * i + 2, :],
                                  bank[3 + i][0:96, :].rearrange("p (h t) -> p h t", h=2), ACT.Copy)
            up.then_inc(W["up_kept"].sem, 1)
            e.wait_ge(*W["up_product"](l, 1))
            e.wait_ge(*W["lat_n"](l))
            for i in range(2):
                up = e.activation(bkh[0:HD, 2 * i:2 * i + 2, :],
                                  bank[5 + i][0:HD, :].rearrange("p (h t) -> p h t", h=2), ACT.Copy)
            up.then_inc(W["up_kept"].sem, 1)
            e.wait_ge(*W["v_product"](l))
            e.activation(bv.rearrange("p t n -> p (t n)"), bank[7][:], ACT.Copy).then_inc(W["v_kept"].sem, 1)
            e.wait_ge(*W["kept"](l, 9))
            e.activation(rtmp2, dgate, ACT.Abs).then_inc(W["d_abs"].sem, 1)
            e.wait_ge(*W["d_abs"](l))
            e.activation(rtmp2, rtmp2, ACT.Exp, scale=-1.0).then_inc(W["d_exp"].sem, 1)
            e.wait_ge(*W["d_exp"](l))
            e.activation(rtmp2, rtmp2, ACT.Ln, bias=one).then_inc(W["d_ln"].sem, 1)
            e.wait_ge(*W["d_min"](l))
            e.activation(rtmp2, rtmp2, ACT.Exp).then_inc(W["d_sig"].sem, 1)
            for hd in range(ATT + 2):
                if hd < ATT:
                    o, st, scale = bank[6 + hd % 2], stats[:, hd * 8:hd * 8 + 8], 96.0 ** -0.5 if hd // 4 == 1 else 1.0
                    e.wait_ge(*W["maxed"](l, hd))
                    if hd >= 2:
                        e.wait_ge(*W["p_turned"](l, hd - 2))
                    e.activation(Pb[hd % 2][:, 0:128], o[:, 0:128], ACT.Exp, bias=st[:, 0:1], scale=scale,
                                 accum_out=st[:, 2:3])
                    e.activation(Pb[hd % 2][:, 128:384], o[:, 128:384], ACT.Exp, bias=st[:, 1:2], scale=scale,
                                 accum_out=st[:, 3:4]).then_inc(W["expd"].sem, 1)
                if 0 <= hd - 1 < ATT:
                    g = hd - 1
                    e.wait_ge(*W["p_turned"](l, g))
                    if g >= 2:
                        e.wait_ge(*W["o_product"](l, g - 2))
                    e.activation(PTb[g % 2], bank[2][:, 0:384], ACT.Copy).then_inc(W["pt_kept"].sem, 1)
                if hd - 2 >= 0 and hd % 2 == 1:
                    g = hd - 2
                    e.wait_ge(*W["o_product"](l, g))
                    e.activation(yhi[:, g // 2, :], bank[1][:, 0:T], ACT.Copy).then_inc(W["o_hi"].sem, 1)
            for k in range(16):
                n = G2 + k
                split_hi(e, unit(r0, u0 + n + 2))
                e.wait_ge(*W["g_abs"](l, k))
                e.activation(gtmp[k % 2], gtmp[k % 2], ACT.Exp, scale=-1.0).then_inc(W["g_exp"].sem, 1)
                e.wait_ge(*W["g_exp"](l, k))
                e.activation(gtmp[k % 2], gtmp[k % 2], ACT.Ln, bias=one).then_inc(W["g_ln"].sem, 1)
                e.wait_ge(*W["g_min"](l, k))
                e.activation(gates[:, k, :], gates[:, k, :], ACT.Exp).then_inc(W["g_sig"].sem, 1)
                if k == 8:
                    e.wait_ge(*W["centred"](l))
                    e.activation(csq, cy, ACT.Square).then_inc(W["c_sq"].sem, 1)
                if k == 10:
                    e.wait_ge(*W["c_var"](l))
                    e.activation(cr[:, 0:T], bank[2][:, 0:T], ACT.Ln, bias=eps, scale=1.0 / 256).then_inc(W["c_ln"].sem, 1)
                    e.wait_ge(*W["c_ln"](l))
                    e.activation(cr[:, 0:T], cr[:, 0:T], ACT.Exp, scale=-0.5).then_inc(W["c_r"].sem, 1)
                if k == 12:
                    e.wait_ge(*W["c_bias"](l))
                    e.activation(csq, cy, ACT.Abs).then_inc(W["c_abs"].sem, 1)
                    e.wait_ge(*W["c_abs"](l))
                    e.activation(csq, csq, ACT.Exp, scale=-1.0).then_inc(W["c_exp"].sem, 1)
                    e.wait_ge(*W["c_exp"](l))
                    e.activation(csq, csq, ACT.Ln, bias=one).then_inc(W["c_l"].sem, 1)
                if k == 13:
                    e.wait_ge(*W["c_min"](l))
                    e.activation(csq, csq, ACT.Exp).then_inc(W["c_sig"].sem, 1)
                if k == 14:
                    e.wait_ge(*W["c_out"](l))
                    e.activation(yhi[:, 6:8, :].rearrange("p c t -> p (c t)"), cy, ACT.Copy).then_inc(W["c_hi"].sem, 1)
            for n in range(4):
                if B2 + n + 2 < O2 + 2:
                    split_hi(e, unit(r0, u0 + B2 + n + 2))
            for g in range(4):
                e.wait_ge(*W["y_added"](l, 12 + g))
                e.activation(xhi[:, 2 * g:2 * g + 2, :], merged2[:, 2 * g:2 * g + 2, :], ACT.Copy).then_inc(W["m_hi"].sem, 1)
            split_hi(e, unit(r0, u0 + O2 + 2))
            split_hi(e, unit(r0, u0 + O2 + 3))

        def mix2_dve(e, l, r0, u0, j):
            split_lo(e, unit(r0, u0))
            split_lo(e, unit(r0, u0 + 1))
            norm_dve(e, j, lambda c: col("g_mix_2", l, c))
            e.wait_ge(*W["cf_hi"](l))
            e.tensor_tensor(cf_lo, cf_raw, cf_hi.bitcast(F32), ALU.subtract).then_inc(W["cf_lo"].sem, 1)
            for n in range(10):
                split_lo(e, unit(r0, u0 + n + 2))
                if n == 0:
                    e.wait_ge(*W["cf_kept"](l))
                    for t in range(TT):
                        up = e.tensor_tensor(cfy[:, t * H2:(t + 1) * H2], cfy[:, t * H2:(t + 1) * H2],
                                             b_forget[:, bass.ds(l * H2, H2)], ALU.add)
                    up.then_inc(W["lf_shift"].sem, 1)
                if n == 1:
                    e.wait_ge(*W["cf_ln"](l))
                    e.scalar_tensor_tensor(lf, cfy, 0.0, cfe, ALU.min, ALU.subtract).then_inc(W["lf"].sem, 1)
                if n == 7:
                    e.wait_ge(*W["lat_r"](l))
                    for c in range(2):
                        e.scalar_tensor_tensor(bqlat[:, c, :], bqlat[:, c, :], col("g_q_lat_2", l, c), lat_r[:, 0:T],
                                               ALU.mult, ALU.mult)
                    e.scalar_tensor_tensor(bkv[:, 0, :], bkv[:, 0, :], col("g_kv_lat_2", l), lat_r[:, T:2 * T],
                                           ALU.mult, ALU.mult).then_inc(W["lat_n"].sem, 1)
            e.wait_ge(*W["up_kept"](l, 1))
            for i in range(2):
                e.wait_ge(*W["turned"](l, i))
                if i:
                    e.wait_ge(*W["rope_done"](l, 0))
                for h in (2 * i, 2 * i + 1):
                    e.tensor_tensor(rtmp[0:96, h % 2 * T:(h % 2 + 1) * T], bank[3 + i][0:96, h % 2 * T:(h % 2 + 1) * T],
                                    sin_t, ALU.mult)
                    up = e.tensor_tensor(bqh[0:96, h, :], bqh[0:96, h, :], cos_t, ALU.mult)
                up.then_inc(W["rope_sin"].sem, 1)
                e.wait_ge(*W["rope_sin"](l, i))
                e.tensor_tensor(bqh[0:96, 2 * i:2 * i + 2, :], bqh[0:96, 2 * i:2 * i + 2, :],
                                rtmp[0:96, :].rearrange("p (h t) -> p h t", h=2), ALU.add).then_inc(W["rope_done"].sem, 1)
            e.wait_ge(*W["turned"](l, 2))
            e.wait_ge(*W["rope_done"](l, 1))
            e.tensor_tensor(rtmp[64:96, 0:T], bank[5][64:96, 0:T], sin_t[64:96, :], ALU.mult)
            e.tensor_tensor(bkv[64:96, 1, :], bkv[64:96, 1, :], cos_t[64:96, :], ALU.mult).then_inc(W["k_tmp"].sem, 1)
            e.wait_ge(*W["k_tmp"](l))
            e.tensor_tensor(bkv[64:96, 1, :], bkv[64:96, 1, :], rtmp[64:96, 0:T], ALU.add).then_inc(W["rope_sin"].sem, 1)
            e.wait_ge(*W["rope_sin"](l, 2))
            for h in range(H2):
                up = e.tensor_copy(bkh[64:96, h, :], bkv[64:96, 1, :])
            up.then_inc(W["rope_done"].sem, 1)
            e.wait_ge(*W["rope_done"](l, 2))
            e.wait_ge(*W["d_ln"](l))
            e.scalar_tensor_tensor(rtmp2, dgate, 0.0, rtmp2, ALU.min, ALU.subtract).then_inc(W["d_min"].sem, 1)
            for hd in range(ATT + 2):
                if hd < ATT:
                    o, st, scale = bank[6 + hd % 2], stats[:, hd * 8:hd * 8 + 8], 96.0 ** -0.5 if hd // 4 == 1 else 1.0
                    e.wait_ge(*W["scores"](l, hd))
                    e.tensor_reduce(st[:, 6:7], o[:, 0:128], AX.X, ALU.max)
                    e.tensor_reduce(st[:, 7:8], o[:, 128:384], AX.X, ALU.max).then_inc(W["rowmax"].sem, 1)
                    e.wait_ge(*W["rowmax"](l, hd))
                    e.tensor_scalar(st[:, 0:2], st[:, 6:8], -scale, None, ALU.mult).then_inc(W["maxed"].sem, 1)
                    e.wait_ge(*W["expd"](l, hd))
                    e.reciprocal(st[:, 4:6], st[:, 2:4]).then_inc(W["inv"].sem, 1)
                    e.wait_ge(*W["inv"](l, hd))
                    e.tensor_scalar(Pb[hd % 2][:, 0:128], Pb[hd % 2][:, 0:128], st[:, 4:5], None, ALU.mult)
                    e.tensor_scalar(Pb[hd % 2][:, 128:384], Pb[hd % 2][:, 128:384], st[:, 5:6], None, ALU.mult)\
                     .then_inc(W["scaled"].sem, 1)
                if hd - 2 >= 0 and hd % 2 == 1:
                    g = hd - 2
                    e.wait_ge(*W["o_hi"](l, g // 2))
                    e.tensor_tensor(ylo[:, g // 2, :], bank[1][:, 0:T], yhi[:, g // 2, :].bitcast(F32), ALU.subtract)\
                     .then_inc(W["o_lo"].sem, 1)
            tap = 0
            for k in range(16):
                n = G2 + k
                split_lo(e, unit(r0, u0 + n + 2))
                wait_unit(e, r0, u0, n)
                if k >= 2:
                    e.wait_ge(*W["g_min"](l, k - 2))
                for b in range(2):
                    m = (2 * k + b)
                    up = e.tensor_scalar(gates[:, k, b * T:(b + 1) * T], bank[6 + k % 2][:, b * T:(b + 1) * T],
                                         gate_bias[:, bass.ds(l * 32 + m, 1)], None, ALU.add)
                up.then_inc(W["g_bias"].sem, 1)
                e.wait_ge(*W["g_bias"](l, k))
                e.scalar_tensor_tensor(gtmp[k % 2], gates[:, k, :], -1.0, gates[:, k, :], ALU.mult, ALU.max)\
                 .then_inc(W["g_abs"].sem, 1)
                for _ in range(4):
                    if tap < CONV_K:
                        if tap == 0:
                            e.wait_ge(*W["u_done"](l))
                            e.wait_ge(*W["p_turned"](l, ATT - 1))
                        else:
                            e.wait_ge(*W["tap"](l, tap - 1))
                        for b in range(2):
                            o, src = cy[:, b * T:(b + 1) * T], dpad[:, b, tap:tap + T]
                            w = dw[:, bass.ds(l * 62 + (tap * 2 + b), 1)]
                            if tap == 0:
                                up = e.tensor_scalar(o, src, w, col("b_dw_2", l, b), ALU.mult, ALU.add)
                            else:
                                up = e.scalar_tensor_tensor(o, src, w, o, ALU.mult, ALU.add)
                        up.then_inc(W["tap"].sem, 1)
                        tap += 1
                e.wait_ge(*W["g_ln"](l, k))
                e.scalar_tensor_tensor(gates[:, k, :], gates[:, k, :], 0.0, gtmp[k % 2], ALU.min, ALU.subtract)\
                 .then_inc(W["g_min"].sem, 1)
                if k == 8:
                    e.wait_ge(*W["mean"](l))
                    for b in range(2):
                        o = cy[:, b * T:(b + 1) * T]
                        up = e.scalar_tensor_tensor(o, bank[2][:, 0:T], -1.0 / 256, o, ALU.mult, ALU.add)
                    up.then_inc(W["centred"].sem, 1)
                if k == 10:
                    e.wait_ge(*W["c_r"](l))
                    for b in range(2):
                        o = cy[:, b * T:(b + 1) * T]
                        up = e.scalar_tensor_tensor(o, o, col("g_conv_ln_2", l, b), cr[:, 0:T], ALU.mult, ALU.mult)
                    up.then_inc(W["c_norm"].sem, 1)
                    e.wait_ge(*W["c_norm"](l))
                    for b in range(2):
                        o = cy[:, b * T:(b + 1) * T]
                        up = e.tensor_scalar(o, o, col("b_conv_ln_2", l, b), None, ALU.add)
                    up.then_inc(W["c_bias"].sem, 1)
                if k == 12:
                    e.wait_ge(*W["c_l"](l))
                    e.scalar_tensor_tensor(csq, cy, 0.0, csq, ALU.min, ALU.subtract).then_inc(W["c_min"].sem, 1)
                if k == 14:
                    e.wait_ge(*W["c_hi"](l))
                    e.tensor_tensor(ylo[:, 6:8, :].rearrange("p c t -> p (c t)"), cy,
                                    yhi[:, 6:8, :].rearrange("p c t -> p (c t)").bitcast(F32), ALU.subtract)\
                     .then_inc(W["c_lo"].sem, 1)
            for n in range(4):
                split_lo(e, unit(r0, u0 + B2 + n + 2))
                for q in range(4):
                    k = 4 * n + q
                    y_ready(e, l, r0, u0, k)
                    e.wait_ge(*W["g_sig"](l, k))
                    m = merged2[:, 2 * q:2 * q + 2, :].rearrange("p c t -> p (c t)")
                    if n == 0:
                        e.tensor_tensor(m, gates[:, k, :], bank[k % 8][:], ALU.mult).then_inc(W["y_scaled"].sem, 1)
                    else:
                        if k >= 6:
                            e.wait_ge(*W["y_added"](l, k - 2))
                        e.tensor_tensor(ytmp2[k % 2], gates[:, k, :], bank[k % 8][:], ALU.mult).then_inc(W["y_scaled"].sem, 1)
            for g in range(4):
                e.wait_ge(*W["m_hi"](l, g))
                e.tensor_tensor(xlo[:, 2 * g:2 * g + 2, :], merged2[:, 2 * g:2 * g + 2, :],
                                xhi[:, 2 * g:2 * g + 2, :].bitcast(F32), ALU.subtract).then_inc(W["m_lo"].sem, 1)
            split_lo(e, unit(r0, u0 + O2 + 2))
            split_lo(e, unit(r0, u0 + O2 + 3))
            add_rows(e, unit(r0, u0 + O2 + 3), 1.0)

        def mix2_pool(e, l, j):
            e.wait_ge(x_new[1], 1 + j)
            finish_waits(e)
            e.memset(dpad[:, :, 0:CONV_K - 1], 0.0).then_inc(W["pads"].sem, 1)
            e.wait_ge(small_in, l * 64 + 64)
            e.wait_ge(*W["pads"](l))
            finish_waits(e)
            e.memset(bias_a[64:128, :, 0:64], MASKED).then_inc(W["bias_masked"].sem, 1)
            e.wait_ge(*W["bias_masked"](l))
            e.wait_ge(*W["lf"](l))
            for h in range(H2):
                if h >= 2:
                    e.wait_ge(*W["scores"](l, 8 + h - 2))
                finish_waits(e)
                for a, (m, c) in enumerate(((le, 0), (ones, 0), (le, 1))):
                    up = e.tensor_scalar(CG[h % 2][:, a * P:(a + 1) * P], m, lf[:, c * H2 + h:c * H2 + h + 1], None,
                                         ALU.mult)
                up.then_inc(W["cg"].sem, 1)
                if h == 1:
                    e.wait_ge(*W["d_sig"](l))
                    u = dpad[:, :, CONV_K - 1:]
                    e.tensor_tensor(u, u, rtmp2.rearrange("p (c t) -> p c t", c=2), ALU.mult).then_inc(W["u_done"].sem, 1)
            e.wait_ge(*W["c_sig"](l))
            e.tensor_tensor(cy, cy, csq, ALU.mult).then_inc(W["c_out"].sem, 1)
            for k in range(16):
                e.wait_ge(*W["y_scaled"](l, k))
                q = k % 4
                m = merged2[:, 2 * q:2 * q + 2, :].rearrange("p c t -> p (c t)")
                if k < 4:
                    e.sem_inc(W["y_added"].sem)
                else:
                    e.wait_ge(*W["y_added"](l, k - 1))
                    e.tensor_tensor(m, m, ytmp2[k % 2], ALU.add).then_inc(W["y_added"].sem, 1)

        def up_unit(r0, u0, i, m=0):
            return unit(r0, u0 + 2 * i - 1, m * 2) if i else unit(r0, u0)

        def down_unit(r0, u0, i, m=0):
            return unit(r0, u0 + 2 * i + 2, m * 2)

        def ffn2_sync(e, l, r0, u0):
            wu, wd = d["w_up_2"], d["w_down_2"]
            load_unit(e, unit(r0, u0), wu[l, :, 0:256].rearrange("(c p) n -> p c n", p=P), as_in)
            with e.Fori(0, 5) as m:
                for k in (1, 2, 3):
                    load_unit(e, up_unit(r0, u0, k, m),
                              wu[l, :, bass.ds(m * 768 + k * 256, 256)].rearrange("(c p) n -> p c n", p=P), as_in)
                    load_unit(e, down_unit(r0, u0, k - 1, m),
                              wd[l, bass.ds(m * 768 + (k - 1) * 256, 256), :].rearrange("(c p) n -> p c n", p=P), as_out)
            load_unit(e, unit(r0, u0 + 31), wd[l, FF2 - 256:FF2, :].rearrange("(c p) n -> p c n", p=P), as_out)

        def h_event(w, l, m, i):
            return w.sem, l * 16 + (m * 3 + (w.start + i + 1))

        def ffn2_pe(e, l, r0, u0, j):
            norm_pe(e, j)
            norm_ready(e, j)
            feature_product(e, unit(r0, u0), GATE, xhi, xlo)

            def down(u, m, i, stop):
                e.wait_ge(*h_event(W["h_hi"], l, m, i))
                e.wait_ge(*h_event(W["h_lo"], l, m, i))
                row_product(e, u, hhi, hlo, stop)

            with e.Fori(0, 5) as m:
                for k in (1, 2, 3):
                    e.wait_ge(*h_event(W["relu"], l, m, k - 1))
                    feature_product(e, up_unit(r0, u0, k, m), GATE, xhi, xlo)
                    down(down_unit(r0, u0, k - 1, m), m, k - 1, False)
            down(unit(r0, u0 + 31), 0, 15, True)

        def ffn2_act(e, l, r0, u0, j):
            split_hi(e, unit(r0, u0))
            split_hi(e, unit(r0, u0 + 1))
            norm_act(e, j, lambda c: col("g_ffn_2", l, c))

            def square(m, i):
                e.wait_ge(*h_event(W["relu"], l, m, i))
                e.wait_ge(*h_event(W["h_lo"], l, m, i - 1))
                e.activation(hbuf, eg, ACT.Square).then_inc(W["square"].sem, 1)

            def split_h(m, i, last_down):
                e.wait_ge(*h_event(W["square"], l, m, i))
                if last_down is not None:
                    s, r = last_down
                    e.wait_ge(multiplied[s], r + 1)
                e.activation(hhi.rearrange("p c t -> p (c t)"), hbuf, ACT.Copy).then_inc(W["h_hi"].sem, 1)

            square(0, 0)
            split_h(0, 0, None)
            with e.Fori(0, 5) as m:
                for k in (1, 2, 3):
                    split_hi(e, unit(r0, u0 + 2 * k, m * 2))
                    split_hi(e, unit(r0, u0 + 2 * k + 1, m * 2))
                    square(m, k)
                    split_h(m, k, down_unit(r0, u0, k - 1, m))

        def ffn2_dve(e, l, r0, u0, j):
            split_lo(e, unit(r0, u0))
            split_lo(e, unit(r0, u0 + 1))
            norm_dve(e, j, lambda c: col("g_ffn_2", l, c))

            def relu(u, m, i):
                s, r = u
                e.wait_ge(multiplied[s], r + 1)
                e.tensor_scalar(eg, GATE[:], 0.0, None, ALU.max).then_inc(W["relu"].sem, 1)

            def split_h(m, i):
                e.wait_ge(*h_event(W["h_hi"], l, m, i))
                e.tensor_tensor(hlo.rearrange("p c t -> p (c t)"), hbuf, hhi.rearrange("p c t -> p (c t)").bitcast(F32),
                                ALU.subtract).then_inc(W["h_lo"].sem, 1)

            relu(unit(r0, u0), 0, 0)
            split_h(0, 0)
            with e.Fori(0, 5) as m:
                for k in (1, 2, 3):
                    split_lo(e, unit(r0, u0 + 2 * k, m * 2))
                    e.wait_ge(*h_event(W["square"], l, m, k - 1))
                    relu(up_unit(r0, u0, k, m), m, k)
                    split_lo(e, unit(r0, u0 + 2 * k + 1, m * 2))
                    split_h(m, k)
            add_rows(e, unit(r0, u0 + 31), 1.0)

        block = ctx.enter_context(nc.Block())
        CONSTS = 8
        LOADS = 12 + len(COL)
        BLOCK_1, BLOCK_2 = DEPTH * SUB_1, DEPTH * SUB_2

        def at_1(l):
            return 1 + l * ROUNDS_1, l * SUB_1

        def at_2(l):
            return 1 + DEPTH * ROUNDS_1 + l * ROUNDS_2, BLOCK_1 + l * SUB_2

        final_gain = arena[:, 4096:4096 + D]
        result = arena[:, 8192:8192 + TT * D].rearrange("p (t d) -> p t d", t=TT)

        @block.sync
        def _(e):
            e.dma_start(x[:], d["x"].rearrange("b (t p) d -> p (b t) d", p=P)).then_inc(loaded, 16)
            e.dma_start(table[:], d["constants"]).then_inc(loaded, 16)
            for l in range(DEPTH):
                e.dma_start(conv_rows[0:96, l, :],
                            d["dn_conv_w"][l].rearrange("k (c p) -> (k c) p", p=P)).then_inc(loaded, 16)
            for name, to in (("dn_dt_bias", dt_bias), ("dn_a_log", a_log), ("b_forget_2", b_forget)):
                e.dma_start(to[:], d[name].rearrange("(o l) h -> o (l h)", o=1).to_broadcast(list(to.shape)))\
                 .then_inc(loaded, 16)
            for name, (a, per) in COL.items():
                v = d[name]
                e.dma_start(rows[a:a + DEPTH * per, :], v.rearrange("l (c p) -> (l c) p", p=P)).then_inc(loaded, 16)
            e.dma_start(gate_rows, d["b_gate_2"].rearrange("l (c p) -> (l c) p", p=P)).then_inc(loaded, 16)
            e.dma_start(dw_rows, d["w_dw_2"].rearrange("l k (c p) -> (l k c) p", p=P)).then_inc(loaded, 16)
            e.dma_start(ext[:, 0:257], d["rel_bias_2"].rearrange("l h n -> (l h) n")).then_inc(loaded, 16)
            e.dma_start(table2, d["constants2"]).then_inc(loaded, 16)
            e.dma_start(positions, d["positions_2"].to_broadcast([32, T])).then_inc(loaded, 16)
            with e.Fori(0, DEPTH) as l:
                r0, j = at_1(l)
                ffn1_sync(e, l, r0, 0, d["ffn1_w_in"], d["ffn1_w_out"])
                mix1_sync(e, l, r0, U_FFN1)
                ffn1_sync(e, l, r0, U_FFN1 + U_MIX1, d["ffn2_w_in"], d["ffn2_w_out"])
            e.wait_ge(x_new[1], 1 + BLOCK_1)
            e.wait_ge(stored, 16)
            e.dma_start(table2, d["constants2"]).then_inc(table2_in, 16)
            with e.Fori(0, DEPTH) as l:
                r0, j = at_2(l)
                mix2_sync(e, l, r0, 0, j)
                ffn2_sync(e, l, r0, U_MIX2)
            e.wait_ge(x_new[1], 1 + BLOCK_1 + BLOCK_2)
            e.dma_start(final_gain, d["g_final_2"].rearrange("(o n) -> o n", o=1).to_broadcast([P, D]))\
             .then_inc(table2_in, 16)
            for t in range(TT):
                e.wait_ge(final_done, t + 1)
                e.dma_start(out[0, t * P:(t + 1) * P, :], result[:, t, :]).then_inc(stored, 16)
            e.wait_ge(stored, 16 + TT * 16)

        @block.gpsimd
        def _(e):
            e.memset(zero[:].bitcast(F32), 0.0).then_inc(consts, 1)
            e.memset(eps, EPS).then_inc(consts, 1)
            e.memset(one, 1.0).then_inc(consts, 1)
            e.memset(ln_scale, -0.5 * math.log(P)).then_inc(consts, 1)
            e.memset(half_pi, 0.5 * math.pi).then_inc(consts, 1)
            e.memset(pre[0][:], 0.0).then_inc(consts, 1)
            e.memset(pre[1][:], 0.0).then_inc(consts, 1)
            e.memset(rotary[:, 0:T], 1.0)
            e.memset(rotary[:, T:2 * T], 0.0).then_inc(consts, 1)
            e.wait_ge(consts, CONSTS)
            e.wait_ge(loaded, 16 * LOADS)
            with e.Fori(0, DEPTH) as l:
                mix1_pool(e, l)
            with e.Fori(0, DEPTH) as l:
                mix2_pool(e, l, at_2(l)[1])

        @block.scalar
        def _(e):
            e.wait_ge(consts, CONSTS)
            e.wait_ge(loaded, 16 * LOADS)
            e.wait_ge(ext_done, 1)
            e.dma_start(bias_rows.rearrange("l h s m -> (l h) s m"), ext.unsqueeze(1).to_broadcast([DEPTH * 4, P, 384]))\
             .then_inc(stored, 16)
            e.wait_ge(angle_step, 9)
            e.activation(sin_t[64:96, :], angle, ACT.Sin).then_inc(rotary_step, 1)
            e.activation(angle_tmp, angle, ACT.Abs).then_inc(rotary_step, 1)
            e.wait_ge(rotary_step, 2)
            e.activation(cos_t[64:96, :], angle_tmp, ACT.Sin, bias=half_pi[64:96, :], scale=-1.0).then_inc(rotary_step, 1)
            e.preload_act_table_set("natural_log_exp_and_others")
            e.wait_ge(cols_done, 1)
            e.wait_ge(stored, 16)
            with e.Fori(0, DEPTH) as l:
                r0, j = at_1(l)
                ffn1_act(e, l, r0, 0, j, l * 2, lambda c: col("ffn1_norm", l, c))
                mix1_act(e, l, r0, U_FFN1, j + 1)
                ffn1_act(e, l, r0, U_FFN1 + U_MIX1, j + 2, l * 2 + 1, lambda c: col("ffn2_norm", l, c))
            with e.Fori(0, DEPTH) as l:
                r0, j = at_2(l)
                mix2_act(e, l, r0, 0, j)
                ffn2_act(e, l, r0, U_MIX2, j + 1)
            rstd_act(e, BLOCK_1 + BLOCK_2)

        @block.vector
        def _(e):
            e.wait_ge(loaded, 16 * LOADS)
            e.wait_ge(cols_t, 1)
            e.tensor_copy(ext[:, 257:384], ext[:, 256:257].to_broadcast([DEPTH * 4, 127])).then_inc(ext_done, 1)
            e.tensor_copy(conv_w[:], bank[1][:, 0:DEPTH * 96])
            e.tensor_copy(gate_bias[:], bank[1][:, 192:256])
            e.tensor_copy(dw[:], bank[1][:, 256:380])
            e.tensor_copy(cols[:], bank[0][:, 0:NV]).then_inc(cols_done, 1)
            for s in (*lo_done, *x_new, h_done, gated, hlo_done, V["ba_lo_done"].sem):
                e.sem_inc(s)
            step = 0

            def angle_after(op):
                nonlocal step
                op.then_inc(angle_step, 1)
                step += 1
                e.wait_ge(angle_step, step)

            angle_after(e.tensor_copy(angle, positions))
            angle_after(e.tensor_scalar(angle, angle, freq[64:96, :], None, ALU.mult))
            angle_after(e.tensor_scalar(turns, angle, 0.5 / math.pi, ROUNDER, ALU.mult, ALU.add))
            angle_after(e.tensor_scalar(turns, turns, -ROUNDER, None, ALU.add))
            for part in TURN:
                angle_after(e.scalar_tensor_tensor(angle, turns, -part, angle, ALU.mult, ALU.add))
            angle_after(e.tensor_scalar(angle, angle, PI, None, ALU.min))
            angle_after(e.tensor_scalar(angle, angle, -PI, None, ALU.max))
            e.wait_ge(cols_done, 1)
            with e.Fori(0, DEPTH) as l:
                r0, j = at_1(l)
                ffn1_dve(e, l, r0, 0, j, l * 2, lambda c: col("ffn1_norm", l, c))
                mix1_dve(e, l, r0, U_FFN1, j + 1)
                ffn1_dve(e, l, r0, U_FFN1 + U_MIX1, j + 2, l * 2 + 1, lambda c: col("ffn2_norm", l, c))
            with e.Fori(0, DEPTH) as l:
                r0, j = at_2(l)
                mix2_dve(e, l, r0, 0, j)
                ffn2_dve(e, l, r0, U_MIX2, j + 1)
            scale_dve(e, BLOCK_1 + BLOCK_2)
            e.wait_ge(table2_in, 32)
            for t in range(TT):
                e.wait_ge(xn_done, (BLOCK_1 + BLOCK_2) * TT + (t + 1))
                e.tensor_tensor(result[:, t, :], xn[:, t, :], final_gain, ALU.mult).then_inc(final_done, 1)

        @block.tensor
        def _(e):
            e.wait_ge(consts, CONSTS)
            e.wait_ge(loaded, 16 * LOADS)
            for s in multiplied:
                e.sem_inc(s)
            for l in range(DEPTH):
                e.transpose(bank[1][:, l * 96:(l + 1) * 96], conv_rows[:, l, :], ident[0:96, 0:96])
            e.transpose(bank[1][:, 192:256], gate_rows, ident[0:64, 0:64])
            e.transpose(bank[1][:, 256:380], dw_rows, ident[0:124, 0:124])
            e.transpose(bank[0][:, 0:NV], rows[0:NV, :], ident[0:NV, 0:NV]).then_inc(cols_t, 1)
            with e.Fori(0, DEPTH) as l:
                r0, j = at_1(l)
                ffn1_pe(e, l, r0, 0, j, l * 2)
                mix1_pe(e, l, r0, U_FFN1, j + 1)
                ffn1_pe(e, l, r0, U_FFN1 + U_MIX1, j + 2, l * 2 + 1)
            e.wait_ge(table2_in, 16)
            with e.Fori(0, DEPTH) as l:
                r0, j = at_2(l)
                mix2_pe(e, l, r0, 0, j)
                ffn2_pe(e, l, r0, U_MIX2, j + 1)


def kernel(**inputs):
    import numpy as np
    from concourse.bacc import Bacc
    from concourse.bass_utils import run_bass_kernel_spmd

    nc = Bacc("TRN2", target_bir_lowering=False, num_devices=1)
    arrays = {name: np.ascontiguousarray(a) for name, a in inputs.items()}
    arrays["constants"] = CONSTANTS
    arrays["constants2"] = CONSTANTS2
    ins = {name: nc.dram_tensor(f"in_{name}", a.shape, mybir.dt.from_np(a.dtype), kind="ExternalInput").ap()
           for name, a in arrays.items()}
    out = nc.dram_tensor("out", (1, T, D), F32, kind="ExternalOutput").ap()
    hybrid_stack_kernel(nc, ins, out)
    got = run_bass_kernel_spmd(nc, [{f"in_{name}": a for name, a in arrays.items()}], core_ids=[0])
    return got.results[0]["out"]
```
